# Optimizing a Trainium2 kernel written in Bass

```python
import jax, jax.numpy as jnp
from jax import lax
import numpy as np
import math

D_MODEL = 1024
BATCH = 1
SEQ = 1024
DEPTH = 1

CHUNK = 64
POOL_WIDTH = D_MODEL // 2
POOL_WINDOWS = (2, 4, 8, 16)
N_POOL_GROUPS = len(POOL_WINDOWS)
POOL_GROUP = POOL_WIDTH // N_POOL_GROUPS
SB_WIDTH = D_MODEL - POOL_WIDTH
SB_HEAD_DIM = 64
SB_HEADS = SB_WIDTH // SB_HEAD_DIM
Q_BLOCK = 128
D_FF = 4 * D_MODEL
PLE_DIM = 256
IN_WIDTH = POOL_WIDTH + 3 * SB_WIDTH
EPS = 1e-6


def rms_norm(x, g):
    xf = x.astype(jnp.float32)
    y = xf * lax.rsqrt(jnp.mean(xf * xf, axis=-1, keepdims=True) + EPS)
    return (y * g.astype(jnp.float32)).astype(x.dtype)

def pool_mixer(u, w_pool, scale):
    b, s, _ = u.shape
    uf = u.astype(jnp.float32).reshape(b, s, N_POOL_GROUPS, POOL_GROUP)
    t = jnp.arange(s)
    outs = []
    for gi, w in enumerate(POOL_WINDOWS):
        ug = uf[:, :, gi]
        c = jnp.cumsum(ug, axis=1)
        c_prev = jnp.pad(c, ((0, 0), (w, 0), (0, 0)))[:, :s]
        cnt = jnp.minimum(t + 1, w).astype(jnp.float32)[None, :, None]
        outs.append((c - c_prev) / cnt - ug)
    d = jnp.stack(outs, axis=2).astype(u.dtype)
    y = jnp.einsum('bsgc,gcd->bsgd', d, w_pool).reshape(b, s, POOL_WIDTH)
    return y * scale

def stick_breaking_attention(q, k, v):
    b, s_len, h, dh = q.shape
    scale = dh ** -0.5
    outs = []
    for start in range(0, s_len, Q_BLOCK):
        end = start + Q_BLOCK
        qb = q[:, start:end]
        kb = k[:, :end]
        vb = v[:, :end]
        z = jnp.einsum('bqhd,bkhd->bhqk', qb, kb,
                       preferred_element_type=jnp.float32) * scale
        t_idx = start + jnp.arange(Q_BLOCK)
        s_idx = jnp.arange(end)
        mask = s_idx[None, :] < t_idx[:, None]
        log_fail = jnp.where(mask, jax.nn.log_sigmoid(-z), 0.0)
        after = lax.cumsum(log_fail, axis=3, reverse=True) - log_fail
        log_a = jax.nn.log_sigmoid(z) + after
        a = jnp.where(mask, jnp.exp(log_a), 0.0)
        outs.append(jnp.einsum('bhqk,bkhd->bqhd', a.astype(v.dtype), vb))
    return jnp.concatenate(outs, axis=1)

def first_inputs(seed: int = 0) -> dict:
    key = jax.random.key(seed)
    ks = jax.random.split(key, 20)
    f32 = jnp.float32

    def nrm(k, shape, fan_in):
        return jax.random.normal(k, shape, f32) * (fan_in ** -0.5)

    def gain(k, shape):
        return 1.0 + 0.05 * jax.random.normal(k, shape, f32)

    return {
        "x": jax.random.normal(ks[0], (BATCH, SEQ, D_MODEL), f32),
        "p": jax.random.normal(ks[1], (DEPTH, BATCH, SEQ, PLE_DIM), f32),
        "g_mix_pre": gain(ks[2], (DEPTH, D_MODEL)),
        "w_in": nrm(ks[3], (DEPTH, D_MODEL, IN_WIDTH), D_MODEL),
        "w_pool": nrm(ks[4], (DEPTH, N_POOL_GROUPS, POOL_GROUP, POOL_GROUP), POOL_GROUP),
        "pool_scale": gain(ks[5], (DEPTH, POOL_WIDTH)),
        "g_sb": gain(ks[6], (DEPTH, SB_WIDTH)),
        "w_out": nrm(ks[7], (DEPTH, D_MODEL, D_MODEL), D_MODEL),
        "g_mix_post": gain(ks[8], (DEPTH, D_MODEL)),
        "g_mlp_pre": gain(ks[9], (DEPTH, D_MODEL)),
        "w_up": nrm(ks[10], (DEPTH, D_MODEL, D_FF), D_MODEL),
        "w_down": nrm(ks[11], (DEPTH, D_FF, D_MODEL), D_FF),
        "g_mlp_post": gain(ks[12], (DEPTH, D_MODEL)),
        "w_ple_gate": nrm(ks[13], (DEPTH, D_MODEL, D_MODEL), D_MODEL),
        "w_ple_proj": nrm(ks[14], (DEPTH, PLE_DIM, D_MODEL), PLE_DIM),
        "g_ple": gain(ks[15], (DEPTH, D_MODEL)),
    }

def first_block(x, p, g_mix_pre, w_in, w_pool, pool_scale, g_sb, w_out, g_mix_post,
              g_mlp_pre, w_up, w_down, g_mlp_post, w_ple_gate, w_ple_proj, g_ple):
    b, s, _ = x.shape
    assert s % CHUNK == 0
    h = x
    for i in range(DEPTH):
        hn = rms_norm(h, g_mix_pre[i])
        proj = hn @ w_in[i]
        u = proj[..., :POOL_WIDTH]
        q, k, v = jnp.split(proj[..., POOL_WIDTH:], 3, axis=-1)
        q = q.reshape(b, s, SB_HEADS, SB_HEAD_DIM)
        k = k.reshape(b, s, SB_HEADS, SB_HEAD_DIM)
        v = v.reshape(b, s, SB_HEADS, SB_HEAD_DIM)

        y_pool = pool_mixer(u, w_pool[i], pool_scale[i])
        o_sb = stick_breaking_attention(q, k, v)
        y_sb = rms_norm(o_sb, jnp.ones((SB_HEAD_DIM,), jnp.float32)).reshape(b, s, SB_WIDTH) * g_sb[i]

        mix = jnp.concatenate([y_pool, y_sb], axis=-1) @ w_out[i]
        h = h + rms_norm(mix, g_mix_post[i])

        m = rms_norm(h, g_mlp_pre[i]) @ w_up[i]
        m = jnp.square(jax.nn.relu(m)) @ w_down[i]
        h = h + rms_norm(m, g_mlp_post[i])

        gate = jax.nn.sigmoid(h @ w_ple_gate[i])
        e = rms_norm(p[i] @ w_ple_proj[i], g_ple[i])
        h = h + gate * e
    return h


MLA_HEADS = 8
MLA_Q_RANK = 384
MLA_KV_RANK = 256
MLA_NOPE = 64
MLA_ROPE = 32
MLA_V = 64
MLA_SCALE = 1.0 / math.sqrt(MLA_NOPE + MLA_ROPE)
ROPE_THETA = 10000.0
FOX_HEADS = 8
FOX_DIM = 64
FOX_SCALE = 1.0 / math.sqrt(FOX_DIM)
D_FF_2 = 2816
CONV_WIDTH = 3
BLOCK_Q = 128
N_ADA = 6

IN_SPLITS = (
    MLA_Q_RANK,
    MLA_KV_RANK,
    MLA_ROPE,
    FOX_HEADS * FOX_DIM,
    FOX_HEADS * FOX_DIM,
    FOX_HEADS * FOX_DIM,
    FOX_HEADS,
    D_MODEL,
    D_MODEL,
)
D_IN = sum(IN_SPLITS)
IN_OFFSETS = tuple(int(v) for v in np.cumsum(IN_SPLITS)[:-1])


def rmsnorm(x, g):
    xf = x.astype(jnp.float32)
    y = xf * lax.rsqrt(jnp.mean(xf * xf, axis=-1, keepdims=True) + EPS)
    return (y * g.astype(jnp.float32)).astype(x.dtype)

def rope(x, positions):
    r = x.shape[-1]
    inv_freq = ROPE_THETA ** (-jnp.arange(0, r, 2, dtype=jnp.float32) / r)
    ang = positions.astype(jnp.float32)[..., None] * inv_freq
    cos = jnp.cos(ang)[:, :, None, :]
    sin = jnp.sin(ang)[:, :, None, :]
    xf = x.astype(jnp.float32)
    x1, x2 = xf[..., : r // 2], xf[..., r // 2:]
    out = jnp.concatenate([x1 * cos - x2 * sin, x2 * cos + x1 * sin], axis=-1)
    return out.astype(x.dtype)

def causal_block_attention(q, k, v, scale, log_cum=None):
    b, s, h, dk = q.shape
    nb = s // BLOCK_Q
    idx = jnp.arange(nb)
    qb = q.reshape(b, nb, BLOCK_Q, h, dk).transpose(1, 0, 2, 3, 4)
    key_pos = jnp.arange(s)
    if log_cum is not None:
        f_keys = log_cum.transpose(0, 2, 1)
        fb = log_cum.reshape(b, nb, BLOCK_Q, h).transpose(1, 0, 2, 3)
        xs = (idx, qb, fb)
    else:
        xs = (idx, qb)

    def one_block(args):
        i, qi = args[0], args[1]
        logits = jnp.einsum('bqhd,bkhd->bhqk', qi, k,
                            preferred_element_type=jnp.float32) * scale
        if log_cum is not None:
            fi = args[2].transpose(0, 2, 1)
            logits = logits + (fi[..., :, None] - f_keys[:, :, None, :])
        q_pos = i * BLOCK_Q + jnp.arange(BLOCK_Q)
        mask = key_pos[None, :] <= q_pos[:, None]
        logits = jnp.where(mask[None, None], logits, -jnp.inf)
        p = jax.nn.softmax(logits, axis=-1)
        return jnp.einsum('bhqk,bkhd->bqhd', p.astype(v.dtype), v)

    out = lax.map(one_block, xs)
    return out.transpose(1, 0, 2, 3, 4).reshape(b, s, h, v.shape[-1])

def hybrid_mixer(h, positions, w_in, q_norm_g, w_uq, kv_norm_g, w_ukv, b_forget,
                 w_o_mla, w_o_fox, w_out):
    b, s, _ = h.shape
    proj = h @ w_in
    cq, ckv, k_rope, fq, fk, fv, f_logit, g_mla, g_fox = jnp.split(proj, IN_OFFSETS, axis=-1)

    q = (rmsnorm(cq, q_norm_g) @ w_uq).reshape(b, s, MLA_HEADS, MLA_NOPE + MLA_ROPE)
    q_nope, q_rope = q[..., :MLA_NOPE], q[..., MLA_NOPE:]
    kv = (rmsnorm(ckv, kv_norm_g) @ w_ukv).reshape(b, s, MLA_HEADS, MLA_NOPE + MLA_V)
    k_nope, v_mla = kv[..., :MLA_NOPE], kv[..., MLA_NOPE:]
    q_rope = rope(q_rope, positions)
    k_rope = rope(k_rope[:, :, None, :], positions)
    q_mla = jnp.concatenate([q_nope, q_rope], axis=-1)
    k_mla = jnp.concatenate(
        [k_nope, jnp.broadcast_to(k_rope, (b, s, MLA_HEADS, MLA_ROPE))], axis=-1)
    o_mla = causal_block_attention(q_mla, k_mla, v_mla, MLA_SCALE).reshape(b, s, MLA_HEADS * MLA_V)

    log_f = jax.nn.log_sigmoid(f_logit.astype(jnp.float32) + b_forget.astype(jnp.float32))
    f_cum = jnp.cumsum(log_f, axis=1)
    o_fox = causal_block_attention(
        fq.reshape(b, s, FOX_HEADS, FOX_DIM), fk.reshape(b, s, FOX_HEADS, FOX_DIM),
        fv.reshape(b, s, FOX_HEADS, FOX_DIM), FOX_SCALE, f_cum).reshape(b, s, FOX_HEADS * FOX_DIM)

    y = jax.nn.sigmoid(g_mla) * (o_mla @ w_o_mla) + jax.nn.sigmoid(g_fox) * (o_fox @ w_o_fox)
    return y @ w_out

def conv_ffn(h, w_up, conv_w, conv_b, w_down):
    s = h.shape[1]
    u = h @ w_up
    up = jnp.pad(u, ((0, 0), (CONV_WIDTH - 1, 0), (0, 0)))
    u = conv_b + sum(conv_w[j] * up[:, j:j + s] for j in range(CONV_WIDTH))
    gate, val = u[..., :D_FF_2], u[..., D_FF_2:]
    return (jax.nn.silu(gate) * val) @ w_down

def modulate(hn, shift, scale):
    return hn * (1.0 + scale[:, None, :]) + shift[:, None, :]

def second_inputs(seed: int = 0) -> dict:
    key = jax.random.key(seed)
    ks = jax.random.split(key, 24)
    nrm = lambda k, shape, fan: jax.random.normal(k, shape, jnp.float32) * (fan ** -0.5)
    L = DEPTH
    x = jax.random.normal(ks[0], (BATCH, SEQ, D_MODEL), jnp.float32)
    c = jax.random.normal(ks[1], (BATCH, D_MODEL), jnp.float32)
    offsets = jax.random.randint(ks[2], (BATCH, 1), 0, 4096, dtype=jnp.int32)
    positions = offsets + jnp.arange(SEQ, dtype=jnp.int32)[None, :]
    return {
        "x": x,
        "c": c,
        "positions": positions,
        "w_ada": 0.5 * nrm(ks[3], (L, D_MODEL, N_ADA * D_MODEL), D_MODEL),
        "b_ada": 0.01 * jax.random.normal(ks[4], (L, N_ADA * D_MODEL), jnp.float32),
        "norm_mix_g": 1.0 + 0.1 * jax.random.normal(ks[5], (L, D_MODEL), jnp.float32),
        "w_in": nrm(ks[6], (L, D_MODEL, D_IN), D_MODEL),
        "q_norm_g": 1.0 + 0.1 * jax.random.normal(ks[7], (L, MLA_Q_RANK), jnp.float32),
        "w_uq": nrm(ks[8], (L, MLA_Q_RANK, MLA_HEADS * (MLA_NOPE + MLA_ROPE)), MLA_Q_RANK),
        "kv_norm_g": 1.0 + 0.1 * jax.random.normal(ks[9], (L, MLA_KV_RANK), jnp.float32),
        "w_ukv": nrm(ks[10], (L, MLA_KV_RANK, MLA_HEADS * (MLA_NOPE + MLA_V)), MLA_KV_RANK),
        "b_forget": jax.random.uniform(ks[11], (L, FOX_HEADS), jnp.float32, 1.0, 6.0),
        "w_o_mla": nrm(ks[12], (L, MLA_HEADS * MLA_V, D_MODEL), MLA_HEADS * MLA_V),
        "w_o_fox": nrm(ks[13], (L, FOX_HEADS * FOX_DIM, D_MODEL), FOX_HEADS * FOX_DIM),
        "w_out": nrm(ks[14], (L, D_MODEL, D_MODEL), D_MODEL),
        "norm_ffn_g": 1.0 + 0.1 * jax.random.normal(ks[15], (L, D_MODEL), jnp.float32),
        "w_up": nrm(ks[16], (L, D_MODEL, 2 * D_FF_2), D_MODEL),
        "conv_w": nrm(ks[17], (L, CONV_WIDTH, 2 * D_FF_2), CONV_WIDTH),
        "conv_b": 0.01 * jax.random.normal(ks[18], (L, 2 * D_FF_2), jnp.float32),
        "w_down": nrm(ks[19], (L, D_FF_2, D_MODEL), D_FF_2),
        "norm_final_g": 1.0 + 0.1 * jax.random.normal(ks[20], (D_MODEL,), jnp.float32),
    }

def second_block(x, c, positions, w_ada, b_ada, norm_mix_g, w_in, q_norm_g, w_uq, kv_norm_g,
              w_ukv, b_forget, w_o_mla, w_o_fox, w_out, norm_ffn_g, w_up, conv_w, conv_b,
              w_down, norm_final_g):
    c_act = jax.nn.silu(c)
    for l in range(DEPTH):
        ada = c_act @ w_ada[l] + b_ada[l]
        sh_m, sc_m, g_m, sh_f, sc_f, g_f = jnp.split(ada, N_ADA, axis=-1)
        h = modulate(rmsnorm(x, norm_mix_g[l]), sh_m, sc_m)
        mix = hybrid_mixer(h, positions, w_in[l], q_norm_g[l], w_uq[l], kv_norm_g[l], w_ukv[l],
                           b_forget[l], w_o_mla[l], w_o_fox[l], w_out[l])
        x = x + g_m[:, None, :] * mix
        h = modulate(rmsnorm(x, norm_ffn_g[l]), sh_f, sc_f)
        x = x + g_f[:, None, :] * conv_ffn(h, w_up[l], conv_w[l], conv_b[l], w_down[l])
    return rmsnorm(x, norm_final_g)


def setup_inputs(seed=0):
    out = dict(first_inputs(seed))
    for name, value in second_inputs(seed + 1).items():
        if name != "x":
            out[name + "_2"] = value
    return out


def reference(
    x, p, g_mix_pre, w_in, w_pool, pool_scale, g_sb, w_out, g_mix_post, g_mlp_pre, w_up, w_down,
    g_mlp_post, w_ple_gate, w_ple_proj, g_ple, c_2, positions_2, w_ada_2, b_ada_2, norm_mix_g_2,
    w_in_2, q_norm_g_2, w_uq_2, kv_norm_g_2, w_ukv_2, b_forget_2, w_o_mla_2, w_o_fox_2, w_out_2,
    norm_ffn_g_2, w_up_2, conv_w_2, conv_b_2, w_down_2, norm_final_g_2,
):
    x = first_block(
        x, p, g_mix_pre, w_in, w_pool, pool_scale, g_sb, w_out, g_mix_post, g_mlp_pre, w_up,
        w_down, g_mlp_post, w_ple_gate, w_ple_proj, g_ple,
    )
    return second_block(
        x, c_2, positions_2, w_ada_2, b_ada_2, norm_mix_g_2, w_in_2, q_norm_g_2, w_uq_2,
        kv_norm_g_2, w_ukv_2, b_forget_2, w_o_mla_2, w_o_fox_2, w_out_2, norm_ffn_g_2, w_up_2,
        conv_w_2, conv_b_2, w_down_2, norm_final_g_2,
    )


_drawn_inputs = setup_inputs


def setup_inputs(seed=0):
    import zlib

    import numpy as np

    out = dict(_drawn_inputs(seed))
    spreads = {}
    factors = {'g_ple': 3.617,
     'b_ada_2': 8.0,
     'norm_mix_g_2': 8.0,
     'q_norm_g_2': 8.0,
     'w_uq_2': 6.013,
     'kv_norm_g_2': 8.0,
     'b_forget_2': 2.967,
     'norm_ffn_g_2': 3.495,
     'conv_b_2': 23.165}
    for name, (base, spread) in spreads.items():
        noise = np.random.default_rng([zlib.crc32(name.encode()), seed]).standard_normal(out[name].shape)
        drawn = base * np.exp(spread * noise) if base else spread * noise
        out[name] = __import__('jax').numpy.asarray(drawn.astype(out[name].dtype))
    for name, factor in factors.items():
        out[name] = (out[name] * factor).astype(out[name].dtype)
    return out
```

```python
from contextlib import ExitStack, contextmanager

import concourse.bass as bass
from concourse import mybir

F32 = mybir.dt.float32
F32R = mybir.dt.float32r
I32 = mybir.dt.int32
ALU = mybir.AluOpType
ACT = mybir.ActivationFunctionType
AX = mybir.AxisListType.X

P = 128
S = 1024
D = 1024
KD = D // P
HALF = 512
EPS = 1e-6
NEG = -1.0e30
SOFTPLUS_TOP = 40.0
MLP1_CHUNKS = 16
MLP2_CHUNKS = 11
ADA_TILES = 48
HD = 64
NOPE, ROPE = 64, 32
MLA_SCALE = (NOPE + ROPE) ** -0.5
START = 4

W_COUNTS = [("qkvu", 16), ("pool", 1), ("out1", 8), ("mlp1", 64), ("ple", 2), ("gate", 8),
            ("in2", 34), ("uq", 4), ("ukv", 2), ("o2", 8), ("out2", 8), ("mlp2", 66)]
W_AT, W_TOTAL = {}, 0
for _name, _n in W_COUNTS:
    W_AT[_name] = W_TOTAL
    W_TOTAL += _n

COLS1, COLS2 = {}, {}


def _columns(table, items):
    at = 0
    for name, n in items:
        table[name] = at
        at += n
    return at


N_COLS1 = _columns(COLS1, [("g_mix_pre", 8), ("pool_scale", 4), ("g_sb", 4), ("g_mix_post", 8),
                           ("g_mlp_pre", 8), ("g_mlp_post", 8), ("g_ple", 8)])
N_COLS2 = _columns(COLS2, [("norm_mix", 8), ("q_norm", 3), ("kv_norm", 2), ("norm_ffn", 8),
                           ("norm_final", 8), ("b_forget", 1), ("inv_freq", 1),
                           ("conv0", 44), ("conv1", 44), ("conv2", 44), ("conv_b", 44)])

STICK = [(c, j, max(0, j - 4 * c) * P) for c in range(2) for j in range(4 * c + 3, -1, -1)]


EXP_LN_TABLES = 6


class Flag:

    def __init__(self, sem, base=0):
        self.sem = sem
        self.base = base

    def at(self, n):
        return self.sem, self.base + n

    def close(self, n):
        self.base += n


@contextmanager
def after(counts):
    for f, n in counts:
        f.base += n
    yield
    for f, n in counts:
        f.base -= n


def two_blocks_kernel(nc, wall, wada, x_t, p_t, c_row, cols1, cols2, b_ada, pos, consts, out):
    ctx = ExitStack()
    with ctx:
        _program(nc, ctx, wall, wada, x_t, p_t, c_row, cols1, cols2, b_ada, pos, consts, out)


def _program(nc, ctx, wall, wada, x_t, p_t, c_row, cols1, cols2, b_ada, pos, consts, out):
    residual_dram = nc.dram_tensor("residual_scratch", (P, KD, S), F32).ap()
    gates_dram = nc.dram_tensor("gates_scratch", (16, P, S), F32).ap()

    KB = 1024
    W0 = 16512
    MAIN = W0 + 24 * KB
    TEMP = MAIN + 160 * KB
    SMALL = TEMP + 20 * KB

    def slots(name, first, n, dt=F32, shape=None):
        return nc.alloc_sbuf_tensor_at(name, shape or [P, n, S], dt, offset=MAIN + first * 4 * KB)

    def temp(name, first, n=1, dt=F32, shape=None):
        return nc.alloc_sbuf_tensor_at(name, shape or [P, n, S], dt, offset=TEMP + first * 4 * KB)

    small_at = [SMALL]

    def small(name, n, dt=F32, rows=P):
        t = nc.alloc_sbuf_tensor_at(name, [rows, n], dt, offset=small_at[0])
        small_at[0] += (4 * n + 31) // 32 * 32
        return t

    w_raw = nc.alloc_sbuf_tensor_at("w_raw", [P, 2, S], F32, offset=W0)
    w_hi = nc.alloc_sbuf_tensor_at("w_hi", [P, 2, S], F32R, offset=W0 + 8 * KB)
    w_lo = nc.alloc_sbuf_tensor_at("w_lo", [P, 2, S], F32R, offset=W0 + 16 * KB)
    ident = small("ident", P, F32R)
    neg_ones = small("neg_ones", P, F32R)
    neg_tri = small("neg_tri", P, F32R)
    mask = small("mask", P, F32R)
    head_ones = small("head_ones", P)
    cols = small("cols", max(N_COLS1, N_COLS2))
    ada = small("ada", ADA_TILES)
    ada_bias = small("ada_bias", ADA_TILES)
    inv_count = small("inv_count", 16)
    stat = small("stat", 8)
    one = inv_count[:, 0:1]
    ident_f = ident[:, :].bitcast(F32)
    neg_ones_f = neg_ones[:, :].bitcast(F32)

    ps = ctx.enter_context(nc.psum_tensor("ps", [P, 8, HALF], F32))

    def pair(n):
        return ps[:, 2 * n:2 * n + 2, :].rearrange("p b n -> p (b n)")

    def sem(name):
        return ctx.enter_context(nc.semaphore(name))

    w_landed = [sem("w_landed_0"), sem("w_landed_1")]
    w_split = sem("w_split")
    w_used = sem("w_used")

    flags, counted, counts = [], [], (10, 18)

    def F(name):
        flags.append(Flag(sem(name), START))
        return flags[-1]

    tile_full = F("tile_full")
    pair_full = F("pair_full")
    pair_free = F("pair_free")
    tile_tmp = F("tile_tmp")
    tile_hi = F("tile_hi")
    tile_lo = F("tile_lo")
    square_ready = F("square_ready")
    square_added = F("square_added")
    stat_full = F("stat_full")
    mean_ready = F("mean_ready")
    rstd_ready = F("rstd_ready")
    loaded = F("loaded")
    stored = F("stored")
    dve_step = F("dve_step")
    act_step = F("act_step")
    pool_step = F("pool_step")
    residual_ready = F("residual_ready")
    evac = F("evac")
    z_full, l_done, sp_done, sph_done, spl_done = (F(n) for n in ("z_full", "l_done", "sp_done", "sph_done", "spl_done"))
    sum_done, suml_done, sumh_done = F("sum_done"), F("suml_done"), F("sumh_done")
    c_full, a_done, ah_done, al_done, pv_done = F("c_full"), F("a_done"), F("ah_done"), F("al_done"), F("pv_done")
    o_free, q_split, v_split = F("o_free"), F("q_split"), F("v_split")
    score_full, max_done, exp_done, p_ready = F("score_full"), F("max_done"), F("exp_done"), F("p_ready")
    acc_zero, emb_ready = F("acc_zero"), F("emb_ready")
    top_done, inverse_done = F("top_done"), F("inverse_done")
    k_in_ready, k_hi, q_hi, v_hi = F("k_in_ready"), F("k_hi"), F("q_hi"), F("v_hi")
    k_split, forget_q = F("k_split"), F("forget_q")
    turn_full, forget_rows = F("turn_full"), [F("forget_rows_0"), F("forget_rows_1")]
    gate_stored = [F("gate_stored_0"), F("gate_stored_1")]
    gates_in = [F("gates_in_0"), F("gates_in_1")]
    ada_landed = [sem("ada_landed_0"), sem("ada_landed_1")]
    ada_used, ada_full, ada_read = F("ada_used"), F("ada_full"), F("ada_read")

    def load_exp_ln():
        load = mybir.InstLoadActFuncSet(name=nc.get_next_instruction_name(), act_func_set_id=EXP_LN_TABLES)
        nc.scalar.add_instruction(load)

    def load_weights(sp, g0, n):
        first, last = g0 + 3, min(g0 + n + 3, W_TOTAL)

        def load(b, slot):
            sp.wait_ge(w_split, 2 * (b - 1))
            sp.dma_start(w_raw[:, slot, :], at_row(wall, b)).then_inc(w_landed[slot], 16)
        pairs = (last - first) // 2
        if pairs > 1:
            with sp.Fori(0, pairs) as i:
                for u in range(2):
                    load(i * 2 + (first + u), (first + u) % 2)
            first += 2 * pairs
        for b in range(first, last):
            load(b, b % 2)

    def split_weights(pool, g0, n):
        first, last = g0 + 1, min(g0 + n + 1, W_TOTAL)

        def split(b, slot, landed):
            pool.wait_ge(w_landed[slot], landed)
            pool.wait_ge(w_used, b + 1)
            nc.gpsimd.tensor_tensor(w_hi[:, slot, :], w_raw[:, slot, :], one.to_broadcast([P, S]),
                                    ALU.mult).then_inc(w_split, 1)
            pool.wait_ge(w_split, b * 2 + 1)
            nc.gpsimd.tensor_tensor(w_lo[:, slot, :], w_raw[:, slot, :],
                                    w_hi[:, slot, :].bitcast(F32), ALU.subtract).then_inc(w_split, 1)
        pairs = (last - first) // 2
        if pairs > 1:
            with pool.Fori(0, pairs) as i:
                for u in range(2):
                    b = first + u
                    split(i * 2 + b, b % 2, i * 16 + 16 * (b // 2 + 1))
            first += 2 * pairs
        for b in range(first, last):
            split(b, b % 2, 16 * (b // 2 + 1))

    def product(pe, slot, at, nk, x_hi, x_lo, k0, banks):
        left = nk * 3
        for k in range(nk):
            for w, xs in ((w_hi, (x_hi, x_lo)), (w_lo, (x_hi,))):
                lhs = w[:, slot, (at + k) * P:(at + k + 1) * P]
                for x in xs:
                    left -= 1
                    for c in range(2):
                        last = nc.tensor.matmul(ps[:, banks + c, :], lhs,
                                                x[:, k0 + k, c * HALF:(c + 1) * HALF],
                                                start=(left == nk * 3 - 1), stop=(left == 0))
        return last

    def use_block(pe, b, slot, nk, per_block, x_hi, x_lo, k0, job, bank_job, ring):
        pe.wait_ge(w_split, b * 2 + 2)
        for m in range(per_block):
            pe.wait_ge(*pair_free.at(job + (m - ring + 1)))
            last = product(pe, slot, m * nk, nk, x_hi, x_lo, k0, 2 * ((bank_job + m) % ring))
            last.then_inc(tile_full.sem if m < per_block - 1 else w_used, 1)

    def first_two(pe, g0, nk, x_hi, x_lo, job, x_flag, x_from=0):
        for u in range(2):
            pe.wait_ge(w_split, (g0 + u) * 2 + 2)
            pe.wait_ge(*pair_free.at(job + u - 1))
        for k in range(nk):
            pe.wait_ge(*x_flag.at(x_from + k + 1))
            for u in range(2):
                for n, (w, x) in enumerate(((w_hi, x_hi), (w_hi, x_lo), (w_lo, x_hi))):
                    for c in range(2):
                        last = nc.tensor.matmul(ps[:, 2 * u + c, :], w[:, (g0 + u) % 2, k * P:(k + 1) * P],
                                                x[:, k, c * HALF:(c + 1) * HALF], start=k == 0 and n == 0,
                                                stop=k == nk - 1 and n == 2)
                if k == nk - 1:
                    last.then_inc(w_used, 1)

    def dense(pe, g0, n, nk, per_block, x_hi, x_lo, ring=2, job0=0, x_flag=None, x_from=0):
        if x_flag is not None and per_block == 1:
            first_two(pe, g0, nk, x_hi, x_lo, job0, x_flag, x_from)
            g0, n, job0, x_flag = g0 + 2, n - 2, job0 + 2, None

        def turn(i):
            for u in range(2):
                if u == 0 and x_flag is not None:
                    pe.wait_ge(*x_flag.at(x_from + nk))
                use_block(pe, i * 2 + (g0 + u), (g0 + u) % 2, nk, per_block, x_hi, x_lo, 0,
                          i * (2 * per_block) + (job0 + u * per_block), u * per_block, ring)
        assert n % 2 == 0 and (2 * per_block) % ring == 0
        turns(pe, n // 2, turn)

    def wait_tile(eng, b, per_block, m, tiles_before):
        if m == per_block - 1:
            eng.wait_ge(w_used, b + 3)
        else:
            eng.wait_ge(*tile_full.at(tiles_before + (m + 1)))

    def turns(eng, n, body):
        if n >= 2:
            with eng.Fori(0, n) as i:
                body(i)
        else:
            for i in range(n):
                body(i)

    def at_tile(t, k):
        return t[:, k, :] if isinstance(k, int) else t[:, bass.ds(k, 1), :].rearrange("p o n -> p (o n)")

    def at_row(t, m):
        return t[m, :, :] if isinstance(m, int) else t[bass.ds(m, 1), :, :].rearrange("o p n -> p (o n)")

    def v_pair(v, p):
        return v[:, :, bass.ds(p * P, P)].rearrange("q b (h n) -> q b h n", h=2)

    sq = temp("square", 0, 2)
    msq = temp("mean_square", 3, 1)
    ln_ms = temp("ln_mean_square", 4, 1)
    rstd = temp("rstd", 2, 1)
    tmp = temp("normed", 0, 2)

    def act_squares(act, src, k0, n, added0=0, ready0=0):
        for k in range(n):
            if k >= 2:
                act.wait_ge(*square_added.at(added0 + k - 1))
            nc.scalar.activation(sq[:, k % 2, :], src[:, k0 + k, :], ACT.Square
                                 ).then_inc(square_ready.sem, 1)

    def dve_sum_squares(dve, n, added0=0, ready0=0):
        for k in range(n):
            dve.wait_ge(*square_ready.at(ready0 + k + 1))
            if k:
                dve.wait_ge(*square_added.at(added0 + k))
                nc.vector.tensor_tensor(msq[:, 0, :], msq[:, 0, :], sq[:, k % 2, :], ALU.add
                                        ).then_inc(square_added.sem, 1)
            else:
                nc.vector.tensor_copy(msq[:, 0, :], sq[:, 0, :]).then_inc(square_added.sem, 1)

    def pe_stat(pe, added, lhs=None, banks=6):
        pe.wait_ge(*square_added.at(added))
        for c in range(2):
            last = nc.tensor.matmul(ps[:, banks + c, :], neg_ones_f if lhs is None else lhs,
                                    msq[:, 0, c * HALF:(c + 1) * HALF], start=True, stop=True)
        last.then_inc(stat_full.sem, 1)

    def pe_sum_squares(pe, n):
        for k in range(n):
            pe.wait_ge(*square_ready.at(k + 1))
            for c in range(2):
                last = nc.tensor.matmul(ps[:, 6 + c, :], neg_ones_f, sq[:, k % 2, c * HALF:(c + 1) * HALF],
                                        start=k == 0, stop=k == n - 1)
            last.then_inc(stat_full.sem if k == n - 1 else square_added.sem, 1)

    def dve_mean(dve, stats, factor, banks=6):
        dve.wait_ge(*stat_full.at(stats))
        nc.vector.tensor_scalar(msq[:, 0, :], pair(banks // 2), factor, EPS, ALU.mult, ALU.add
                                ).then_inc(mean_ready.sem, 1)

    def act_rstd(act, n):
        load_exp_ln()
        act.wait_ge(*mean_ready.at(n))
        nc.scalar.activation(ln_ms[:, 0, :], msq[:, 0, :], ACT.Ln).then_inc(rstd_ready.sem, 1)
        act.wait_ge(*rstd_ready.at(2 * n - 1))
        nc.scalar.activation(rstd[:, 0, :], ln_ms[:, 0, :], ACT.Exp, scale=-0.5
                             ).then_inc(rstd_ready.sem, 1)

    def dve_apply(dve, src, k0, n, gain, lo_out, hi_out, o0, shift=None, done=0):
        def lo(k):
            dve.wait_ge(*tile_hi.at(done + k + 1))
            if shift is None:
                nc.vector.tensor_tensor(lo_out[:, o0 + k, :], tmp[:, k % 2, :],
                                        hi_out[:, o0 + k, :].bitcast(F32), ALU.subtract
                                        ).then_inc(tile_lo.sem, 1)
            else:
                nc.vector.scalar_tensor_tensor(
                    out=lo_out[:, o0 + k, :], in0=tmp[:, k % 2, :], scalar=shift(k),
                    in1=hi_out[:, o0 + k, :].bitcast(F32), op0=ALU.add, op1=ALU.subtract
                ).then_inc(tile_lo.sem, 1)
        for k in range(n):
            if k >= 2:
                dve.wait_ge(*tile_lo.at(done + k - 1))
            nc.vector.scalar_tensor_tensor(out=tmp[:, k % 2, :], in0=src[:, k0 + k, :], scalar=gain(k),
                                           in1=rstd[:, 0, :], op0=ALU.mult, op1=ALU.mult
                                           ).then_inc(tile_tmp.sem, 1)
            if k:
                lo(k - 1)
        lo(n - 1)

    def act_apply(act, n, hi_out, o0, shift=None, done=0):
        for k in range(n):
            act.wait_ge(*tile_tmp.at(done + k + 1))
            nc.scalar.activation(hi_out[:, o0 + k, :], tmp[:, k % 2, :], ACT.Identity,
                                 bias=0.0 if shift is None else shift(k)).then_inc(tile_hi.sem, 1)

    res = slots("residual", 16, 8)
    x_hi = slots("x_hi", 0, 8, F32R)
    x_lo = slots("x_lo", 8, 8, F32R)
    raw1 = slots("qkvu_raw", 24, 16)
    Q1, K1, V1, U1 = 0, 4, 8, 12
    v_tok1 = slots("v_tokens_1", 16, 4, F32, [P, 8, HALF])
    C1, C2 = (lambda name, k: cols[:, COLS1[name] + k:COLS1[name] + k + 1]), \
             (lambda name, k: cols[:, COLS2[name] + k:COLS2[name] + k + 1])

    cst = temp("constants_in", 0, 1, F32, [P, 6, P])
    with nc.Block() as block:
        @block.sync
        def _(sp):
            sp.sem_inc(w_used, 2)
            for f in flags:
                sp.sem_inc(f.sem, START)

    with nc.Block() as block:
        @block.sync
        def _(sp):
            sp.dma_start(w_raw[:, 0, :], wall[0, :, :]).then_inc(w_landed[0], 16)
            sp.dma_start(w_raw[:, 1, :], wall[1, :, :]).then_inc(w_landed[1], 16)
            sp.dma_start(cst[:, :, :], consts[:, 0:6 * P].rearrange("p (a b) -> p a b", b=P)
                         ).then_inc(loaded.sem, 16)
            sp.dma_start(inv_count[:, :], consts[:, 6 * P:6 * P + 16]).then_inc(loaded.sem, 16)
            sp.dma_start(cols[:, 0:N_COLS1], cols1).then_inc(loaded.sem, 16)
            sp.dma_start(ada_bias[:, :], b_ada).then_inc(loaded.sem, 16)
            for h in range(2):
                sp.dma_start(res[:, 4 * h:4 * h + 4, :], x_t[:, 4 * h:4 * h + 4, :]).then_inc(loaded.sem, 16)
            sp.wait_ge(w_split, 2)
            sp.dma_start(w_raw[:, 0, :], wall[2, :, :]).then_inc(w_landed[0], 16)
            sp.wait_ge(*loaded.at(96))

        @block.gpsimd
        def _(pool):
            pool.wait_ge(w_landed[0], 16)
            nc.gpsimd.tensor_scalar(w_hi[:, 0, :], w_raw[:, 0, :], 1.0, 1.0, ALU.mult, ALU.mult
                                    ).then_inc(w_split, 1)
            pool.wait_ge(w_split, 1)
            nc.gpsimd.tensor_tensor(w_lo[:, 0, :], w_raw[:, 0, :], w_hi[:, 0, :].bitcast(F32),
                                    ALU.subtract).then_inc(w_split, 1)

        @block.vector
        def _(dve):
            dve.wait_ge(*loaded.at(96))
            for n, t in enumerate((ident, neg_ones, neg_tri, mask, head_ones)):
                nc.vector.tensor_copy(t[:, :], cst[:, n, :]).then_inc(dve_step.sem, 1)
    loaded.close(96)
    dve_step.close(5)

    G = W_AT["qkvu"]
    with nc.Block() as block:
        @block.sync
        def _(sp):
            load_weights(sp, G, 16)

        @block.gpsimd
        def _(pool):
            split_weights(pool, G, 16)

        @block.scalar
        def _(act):
            act_squares(act, res, 0, 8)
            act_rstd(act, 1)
            act_apply(act, 8, x_hi, 0)

        @block.tensor
        def _(pe):
            pe_sum_squares(pe, 8)
            dense(pe, G, 16, 8, 1, x_hi, x_lo, x_flag=tile_lo)
            for m in range(4):
                pe.wait_ge(*pair_free.at(16 + m - 1))
                for b in range(8):
                    last = nc.tensor.transpose(ps[:, 2 * (m % 2) + b // 4, (b % 4) * P:(b % 4 + 1) * P],
                                               raw1[:, V1 + m, b * P:(b + 1) * P], ident_f)
                last.then_inc(evac.sem, 1)

        @block.vector
        def _(dve):
            dve_mean(dve, 1, -1.0 / D)
            dve.wait_ge(*rstd_ready.at(2))
            dve_apply(dve, res, 0, 8, lambda k: C1("g_mix_pre", k), x_lo, x_hi, 0)

            def body(i):
                for u in range(2):
                    wait_tile(dve, i * 2 + (G + u), 1, 0, 0)
                    nc.vector.tensor_copy(at_tile(raw1, i * 2 + u), pair(u)).then_inc(pair_free.sem, 1)
            turns(dve, 8, body)
            for m in range(4):
                dve.wait_ge(*evac.at(m + 1))
                nc.vector.tensor_copy(v_tok1[:, :, m * P:(m + 1) * P],
                                      pair(m % 2).rearrange("p (b n) -> p b n", n=P)
                                      ).then_inc(pair_free.sem, 1)
    for f, n in ((square_ready, 8), (square_added, 7), (stat_full, 1), (mean_ready, 1), (rstd_ready, 2),
                 (tile_tmp, 8), (tile_hi, 8), (tile_lo, 8), (pair_free, 20), (evac, 4)):
        f.close(n)

    y_hi, y_lo = x_hi, x_lo
    d_hi = slots("pool_d_hi", 4, 2, F32R)
    d_lo = slots("pool_d_lo", 6, 2, F32R)
    win = temp("window_sums", 0, 2)
    dif = temp("pool_difference", 2, 2)
    yp = temp("pool_out", 4, 1)
    G = W_AT["pool"]
    with nc.Block() as block:
        @block.sync
        def _(sp):
            load_weights(sp, G, 1)

        @block.gpsimd
        def _(pool):
            split_weights(pool, G, 1)

        def group_done(eng, g):
            if g == 3:
                eng.wait_ge(w_used, G + 3)
            else:
                eng.wait_ge(*tile_full.at(g + 1))

        @block.scalar
        def _(act):
            for g in range(4):
                act.wait_ge(*tile_tmp.at(g + 1))
                if g >= 2:
                    group_done(act, g - 2)
                nc.scalar.activation(d_hi[:, g % 2, :], dif[:, g % 2, :], ACT.Identity
                                     ).then_inc(tile_hi.sem, 1)
            for g in range(4):
                group_done(act, g)
                if g:
                    act.wait_ge(*pair_free.at(g))
                nc.scalar.activation(yp[:, 0, :], pair(g), ACT.Identity, scale=C1("pool_scale", g)
                                     ).then_inc(act_step.sem, 1)
                act.wait_ge(*act_step.at(2 * g + 1))
                nc.scalar.activation(y_hi[:, g, :], yp[:, 0, :], ACT.Identity).then_inc(act_step.sem, 1)

        @block.tensor
        def _(pe):
            pe.wait_ge(w_split, 2 * G + 2)
            for g in range(4):
                pe.wait_ge(*tile_lo.at(g + 1))
                left = 6
                for w, xs in ((w_hi, (d_hi, d_lo)), (w_lo, (d_hi,))):
                    for x in xs:
                        for c in range(2):
                            left -= 1
                            last = nc.tensor.matmul(ps[:, 2 * g + c, :], w[:, G % 2, g * P:(g + 1) * P],
                                                    x[:, g % 2, c * HALF:(c + 1) * HALF],
                                                    start=left >= 4, stop=left < 2)
                last.then_inc(w_used if g == 3 else tile_full.sem, 1)

        @block.vector
        def _(dve):
            n = 0
            for g in range(4):
                u = raw1[:, U1 + g, :]
                src = u
                for e in range(g + 1):
                    dst = win[:, e % 2, :]
                    w = 1 << e
                    nc.vector.tensor_copy(dst[:, 0:w], src[:, 0:w]).then_inc(dve_step.sem, 1)
                    nc.vector.tensor_tensor(dst[:, w:S], src[:, w:S], src[:, 0:S - w], ALU.add
                                            ).then_inc(dve_step.sem, 1)
                    n += 2
                    dve.wait_ge(*dve_step.at(n))
                    src = dst
                w = 2 << g
                nc.vector.tensor_tensor(src[:, 0:w], src[:, 0:w], inv_count[:, 0:w], ALU.mult
                                        ).then_inc(dve_step.sem, 1)
                n += 1
                dve.wait_ge(*dve_step.at(n))
                if g >= 2:
                    dve.wait_ge(*tile_lo.at(g - 1))
                nc.vector.tensor_tensor(dif[:, g % 2, 0:w], src[:, 0:w], u[:, 0:w], ALU.subtract
                                        ).then_inc(dve_step.sem, 1)
                n += 1
                dve.wait_ge(*dve_step.at(n))
                nc.vector.scalar_tensor_tensor(out=dif[:, g % 2, w:S], in0=src[:, w:S], scalar=1.0 / w,
                                               in1=u[:, w:S], op0=ALU.mult, op1=ALU.subtract
                                               ).then_inc(tile_tmp.sem, 1)
                dve.wait_ge(*tile_hi.at(g + 1))
                nc.vector.tensor_tensor(d_lo[:, g % 2, :], dif[:, g % 2, :], d_hi[:, g % 2, :].bitcast(F32),
                                        ALU.subtract).then_inc(tile_lo.sem, 1)
            for g in range(4):
                dve.wait_ge(*act_step.at(2 * g + 2))
                nc.vector.tensor_tensor(y_lo[:, g, :], yp[:, 0, :], y_hi[:, g, :].bitcast(F32),
                                        ALU.subtract).then_inc(pair_free.sem, 1)
    for f, n in ((tile_tmp, 4), (tile_hi, 4), (tile_lo, 4), (tile_full, 3), (act_step, 8),
                 (pair_free, 4), (dve_step, 2 * (1 + 2 + 3 + 4) + 8)):
        f.close(n)

    qk_hi = slots("stick_qk_hi", 4, 2, F32R)
    qk_lo = slots("stick_qk_lo", 6, 2, F32R)
    vs1 = slots("stick_v_split", 20, 2, F32R, [P, 8, 2, P])
    e_buf = slots("stick_l", 13, 1, F32, [P, 2, HALF])
    sp_buf = slots("stick_sp", 14, 1, F32, [P, 2, HALF])
    sph = slots("stick_sp_hi", 15, 1, F32R, [P, 2, HALF])
    spl = slots("stick_sp_lo", 12, 1, F32R, [P, 2, HALF])
    smh = slots("stick_sum_hi", 22, 1, F32R, [P, 2, HALF])
    sml = slots("stick_sum_lo", 23, 1, F32R, [P, 2, HALF])
    a_buf = temp("stick_a", 0, 1, F32, [P, 2, HALF])
    ah = temp("stick_a_hi", 1, 1, F32R, [P, 2, HALF])
    al = temp("stick_a_lo", 2, 1, F32R, [P, 2, HALF])
    sm = temp("stick_sum", 3, 1, F32, [P, 2, HALF])
    o_low = temp("stick_o_low", 4, 1, F32, [HD, HALF])

    def o_copy(act, n, c):
        act.wait_ge(*o_free.at(n))
        nc.scalar.activation(o_low[:, 0:HALF], ps[HD:P, 6 + c, :], ACT.Copy).then_inc(evac.sem, 1)

    def o_add(dve, n, h, c, o_out, tile):
        dve.wait_ge(*evac.at(n + 1))
        dst = (o_out[h * HD:(h + 1) * HD, bass.ds(tile, 1), c * HALF:(c + 1) * HALF]
               .rearrange("q o n -> q (o n)"))
        nc.vector.tensor_tensor(dst, ps[0:HD, 6 + c, :], o_low[:, 0:HALF], ALU.add
                                ).then_inc(o_free.sem, 1)

    NS = 2 * len(STICK)
    with nc.Block() as block:
        def step(k):
            h, m = divmod(k, len(STICK))
            return (h, *STICK[m])

        def first_of_chunk(k):
            return step(k)[2] == 4 * step(k)[1] + 3

        @block.scalar
        def _(act):
            load_exp_ln()

            def body(p):
                def soft(k):
                    _, c, j, off = step(k)
                    act.wait_ge(*z_full.at(p * NS + (k + 1)))
                    act.wait_ge(*sp_done.at(p * NS + (k - 1)))
                    nc.scalar.activation(e_buf[:, k % 2, off:HALF], ps[:, k % 4, off:HALF], ACT.Exp
                                         ).then_inc(act_step.sem, 1)
                    act.wait_ge(*act_step.at(p * NS + (k + 1)))
                    nc.scalar.activation(e_buf[:, k % 2, off:HALF], e_buf[:, k % 2, off:HALF], ACT.Ln,
                                         bias=1.0).then_inc(l_done.sem, 1)
                act.wait_ge(*pv_done.at(p * NS))
                for n, (t, s) in enumerate(((Q1, HD ** -0.5), (K1, 1.0))):
                    nc.scalar.activation(qk_hi[:, n, :], at_tile(raw1, p + t), ACT.Copy, scale=s
                                         ).then_inc(tile_hi.sem, 1)
                nc.scalar.activation(vs1[:, :, :, 0:HD], v_pair(v_tok1, p), ACT.Copy).then_inc(tile_hi.sem, 1)
                soft(0)
                for k in range(NS):
                    h, c, j, off = step(k)
                    if k + 1 < NS:
                        soft(k + 1)
                    act.wait_ge(*sum_done.at(p * NS + (k + 1)))
                    act.wait_ge(*c_full.at(p * NS + k))
                    nc.scalar.activation(smh[:, k % 2, off:HALF], sm[:, k % 2, off:HALF], ACT.Identity
                                         ).then_inc(sumh_done.sem, 1)
                    act.wait_ge(*c_full.at(p * NS + (k + 1)))
                    act.wait_ge(*al_done.at(p * NS + (k - 1)))
                    nc.scalar.activation(a_buf[:, k % 2, off:HALF], ps[:, k % 4, off:HALF], ACT.Exp
                                         ).then_inc(a_done.sem, 1)
                    act.wait_ge(*a_done.at(p * NS + (k + 1)))
                    act.wait_ge(*pv_done.at(p * NS + (k - 1)))
                    nc.scalar.activation(ah[:, k % 2, off:HALF], a_buf[:, k % 2, off:HALF], ACT.Identity
                                         ).then_inc(ah_done.sem, 1)
                    if j == 0:
                        act.wait_ge(*pv_done.at(p * NS + (k + 1)))
                        o_copy(act, p * 4 + (2 * h + c), c)
            turns(act, 4, body)

        @block.vector
        def _(dve):
            def body(p):
                def soft(k):
                    _, c, j, off = step(k)
                    cs = slice(off, HALF)
                    dve.wait_ge(*l_done.at(p * NS + (k + 1)))
                    dve.wait_ge(*sum_done.at(p * NS + (k - 1)))
                    nc.vector.scalar_tensor_tensor(out=sp_buf[:, k % 2, cs], in0=e_buf[:, k % 2, cs],
                                                   scalar=SOFTPLUS_TOP, in1=ps[:, k % 4, cs],
                                                   op0=ALU.min, op1=ALU.max).then_inc(sp_done.sem, 1)
                    dve.wait_ge(*sp_done.at(p * NS + (k + 1)))
                    dve.wait_ge(*c_full.at(p * NS + (k - 1)))
                    nc.vector.tensor_copy(sph[:, k % 2, cs], sp_buf[:, k % 2, cs]).then_inc(sph_done.sem, 1)
                    dve.wait_ge(*sph_done.at(p * NS + (k + 1)))
                    nc.vector.tensor_tensor(spl[:, k % 2, cs], sp_buf[:, k % 2, cs],
                                            sph[:, k % 2, cs].bitcast(F32), ALU.subtract
                                            ).then_inc(spl_done.sem, 1)
                for n, (t, s) in enumerate(((Q1, HD ** -0.5), (K1, 1.0))):
                    dve.wait_ge(*tile_hi.at(p * 3 + (n + 1)))
                    nc.vector.scalar_tensor_tensor(out=qk_lo[:, n, :], in0=at_tile(raw1, p + t), scalar=s,
                                                   in1=qk_hi[:, n, :].bitcast(F32), op0=ALU.mult,
                                                   op1=ALU.subtract).then_inc(q_split.sem, 1)
                dve.wait_ge(*tile_hi.at(p * 3 + 3))
                nc.vector.tensor_tensor(vs1[:, :, :, HD:P], v_pair(v_tok1, p),
                                        vs1[:, :, :, 0:HD].bitcast(F32), ALU.subtract
                                        ).then_inc(v_split.sem, 1)
                soft(0)
                for k in range(NS):
                    h, c, j, off = step(k)
                    if k + 1 < NS:
                        soft(k + 1)
                    dve.wait_ge(*ah_done.at(p * NS + (k + 1)))
                    nc.vector.tensor_tensor(al[:, k % 2, off:HALF], a_buf[:, k % 2, off:HALF],
                                            ah[:, k % 2, off:HALF].bitcast(F32), ALU.subtract
                                            ).then_inc(al_done.sem, 1)
                    if j == 0:
                        o_add(dve, p * 4 + (2 * h + c), h, c, raw1, p)
            turns(dve, 4, body)

        @block.gpsimd
        def _(pool):
            def body(p):
                def low(k):
                    off = step(k)[3]
                    pool.wait_ge(*sumh_done.at(p * NS + (k + 1)))
                    nc.gpsimd.tensor_tensor(sml[:, k % 2, off:HALF], sm[:, k % 2, off:HALF],
                                            smh[:, k % 2, off:HALF].bitcast(F32), ALU.subtract
                                            ).then_inc(suml_done.sem, 1)
                for k in range(NS):
                    h, c, j, off = step(k)
                    pool.wait_ge(*sumh_done.at(p * NS + (k - 1)))
                    pool.wait_ge(*suml_done.at(p * NS + (k - 1)))
                    pool.wait_ge(*sum_done.at(p * NS + k))
                    pool.wait_ge(*sp_done.at(p * NS + (k + 1)))
                    old, new = off, slice(off, off + P)
                    if j >= 4 * c:
                        new_sum = nc.gpsimd.tensor_tensor(sm[:, k % 2, new], sp_buf[:, k % 2, new],
                                                          one.to_broadcast([P, P]), ALU.mult)
                        old += P
                    if old < HALF:
                        new_sum = nc.gpsimd.tensor_tensor(sm[:, k % 2, old:HALF], sm[:, (k - 1) % 2, old:HALF],
                                                          sp_buf[:, k % 2, old:HALF], ALU.add)
                    new_sum.then_inc(sum_done.sem, 1)
                    low(k)
            turns(pool, 4, body)

        @block.tensor
        def _(pe):
            def body(p):
                def scores(k):
                    h, c, j, off = step(k)
                    r = slice(h * HD, (h + 1) * HD)
                    pe.wait_ge(*a_done.at(p * NS + (k - 3)))
                    qs = slice(c * HALF + off, (c + 1) * HALF)
                    ks = slice(j * P, (j + 1) * P)
                    for n, (a, b) in enumerate(((qk_hi, qk_hi), (qk_hi, qk_lo), (qk_lo, qk_hi))):
                        last = nc.tensor.matmul(ps[:, k % 4, off:HALF], a[r, 1, ks], b[r, 0, qs],
                                                start=n == 0, stop=n == 2)
                        if n == 0 and j >= 4 * c:
                            nc.tensor.matmul(ps[:, k % 4, off:off + P], ident[:, :], mask[:, :],
                                             start=False, stop=False, skip_group_check=True)
                    last.then_inc(z_full.sem, 1)

                def sums(k):
                    h, c, j, off = step(k)
                    pe.wait_ge(*spl_done.at(p * NS + (k + 1)))
                    for n, t in enumerate((sph, spl)):
                        last = nc.tensor.matmul(ps[:, k % 4, off:HALF], neg_tri[:, :], t[:, k % 2, off:HALF],
                                                start=False, stop=True, skip_group_check=True)
                    if not first_of_chunk(k):
                        pe.wait_ge(*suml_done.at(p * NS + k))
                        o = step(k - 1)[3]
                        for t in (smh, sml):
                            last = nc.tensor.matmul(ps[:, k % 4, o:HALF], neg_ones[:, :],
                                                    t[:, (k - 1) % 2, o:HALF], start=False, stop=True,
                                                    skip_group_check=True)
                    last.then_inc(c_full.sem, 1)

                def values(k):
                    h, c, j, off = step(k)
                    pe.wait_ge(*al_done.at(p * NS + (k + 1)))
                    f = first_of_chunk(k)
                    if f:
                        pe.wait_ge(*o_free.at(p * 4 + (2 * h + c - 1)))
                    for n, t in enumerate((ah, al)):
                        last = nc.tensor.matmul(ps[:, 6 + c, off:HALF], vs1[:, j, h, :],
                                                t[:, k % 2, off:HALF], start=f and n == 0,
                                                stop=j == 0 and n == 1, skip_group_check=True)
                    last.then_inc(pv_done.sem, 1)
                pe.wait_ge(*q_split.at(p * 2 + 2))
                pe.wait_ge(*v_split.at(p + 1))
                scores(0)
                scores(1)
                for k in range(NS):
                    if k + 2 < NS:
                        scores(k + 2)
                    sums(k)
                    if k:
                        values(k - 1)
                values(NS - 1)
            turns(pe, 4, body)
    for f, n in ((z_full, NS), (l_done, NS), (sp_done, NS), (sph_done, NS), (spl_done, NS), (sum_done, NS),
                 (suml_done, NS), (sumh_done, NS), (c_full, NS), (a_done, NS), (ah_done, NS), (al_done, NS),
                 (pv_done, NS), (act_step, NS), (tile_hi, 3), (q_split, 2), (v_split, 1), (evac, 4),
                 (o_free, 4)):
        f.close(4 * n)

    mix = slots("mix", 24, 8)
    hms = temp("head_mean_square", 2, 2)
    G = W_AT["out1"]

    def mix_squares(act, g0, n, sq0):
        for k in range(n):
            wait_tile(act, g0 + k, 1, 0, 0)
            act.wait_ge(*square_added.at(sq0 + k - 1))
            nc.scalar.activation(sq[:, k % 2, :], pair(k % 2), ACT.Square).then_inc(square_ready.sem, 1)

    def mix_evac(dve, n, dst, sq0, added0):
        for k in range(n):
            dve.wait_ge(*square_ready.at(sq0 + k + 1))
            if k:
                dve.wait_ge(*square_added.at(added0 + k))
                nc.vector.tensor_tensor(msq[:, 0, :], msq[:, 0, :], sq[:, k % 2, :], ALU.add
                                        ).then_inc(square_added.sem, 1)
            else:
                nc.vector.tensor_copy(msq[:, 0, :], sq[:, 0, :]).then_inc(square_added.sem, 1)
            nc.vector.tensor_copy(dst[:, k, :], pair(k % 2)).then_inc(pair_free.sem, 1)

    with nc.Block() as block:
        @block.sync
        def _(sp):
            for h in range(2):
                sp.dma_start(res[:, 4 * h:4 * h + 4, :], x_t[:, 4 * h:4 * h + 4, :]).then_inc(loaded.sem, 16)
            load_weights(sp, G, 8)
            sp.wait_ge(*loaded.at(32))

        @block.gpsimd
        def _(pool):
            split_weights(pool, G, 8)

        @block.scalar
        def _(act):
            def square(k):
                if k >= 2:
                    act.wait_ge(*stat_full.at(k - 1))
                nc.scalar.activation(sq[:, k % 2, :], raw1[:, k, :], ACT.Square).then_inc(square_ready.sem, 1)
            square(0)
            square(1)
            for k in range(4):
                act.wait_ge(*mean_ready.at(k + 1))
                nc.scalar.activation(hms[:, k % 2, :], hms[:, k % 2, :], ACT.Ln).then_inc(act_step.sem, 1)
                act.wait_ge(*act_step.at(k + 1))
                nc.scalar.activation(hms[:, k % 2, :], hms[:, k % 2, :], ACT.Exp, scale=-0.5
                                     ).then_inc(rstd_ready.sem, 1)
                if k < 2:
                    square(k + 2)
                act.wait_ge(*tile_tmp.at(k + 1))
                nc.scalar.activation(y_hi[:, 4 + k, :], raw1[:, k, :], ACT.Identity).then_inc(tile_hi.sem, 1)
            act.wait_ge(*stat_full.at(4))
            mix_squares(act, G, 8, 0)

        @block.tensor
        def _(pe):
            for k in range(4):
                pe.wait_ge(*square_ready.at(k + 1))
                if k >= 2:
                    pe.wait_ge(*mean_ready.at(k - 1))
                for c in range(2):
                    last = nc.tensor.matmul(ps[:, 4 + 2 * (k % 2) + c, :], head_ones[:, :],
                                            sq[:, k % 2, c * HALF:(c + 1) * HALF], start=True, stop=True)
                last.then_inc(stat_full.sem, 1)
            dense(pe, G, 8, 8, 1, y_hi, y_lo, x_flag=tile_lo, x_from=-4)

        @block.vector
        def _(dve):
            def mean(k):
                dve.wait_ge(*stat_full.at(k + 1))
                if k >= 2:
                    dve.wait_ge(*tile_tmp.at(k - 1))
                nc.vector.tensor_scalar(hms[:, k % 2, :], pair(2 + k % 2), 1.0 / HD, EPS, ALU.mult, ALU.add
                                        ).then_inc(mean_ready.sem, 1)
            mean(0)
            for k in range(4):
                if k < 3:
                    mean(k + 1)
                dve.wait_ge(*rstd_ready.at(k + 1))
                nc.vector.scalar_tensor_tensor(out=raw1[:, k, :], in0=raw1[:, k, :], scalar=C1("g_sb", k),
                                               in1=hms[:, k % 2, :], op0=ALU.mult, op1=ALU.mult
                                               ).then_inc(tile_tmp.sem, 1)
                dve.wait_ge(*tile_hi.at(k + 1))
                nc.vector.tensor_tensor(y_lo[:, 4 + k, :], raw1[:, k, :], y_hi[:, 4 + k, :].bitcast(F32),
                                        ALU.subtract).then_inc(tile_lo.sem, 1)
            mix_evac(dve, 8, mix, 4, 0)
    for f, n in ((square_ready, 12), (square_added, 8), (stat_full, 4), (mean_ready, 4), (rstd_ready, 4),
                 (tile_tmp, 4), (tile_hi, 4), (tile_lo, 4), (act_step, 4), (pair_free, 8), (loaded, 32)):
        f.close(n)

    acc = mix
    h_hi = slots("hidden_hi", 32, 4, F32R)
    h_lo = slots("hidden_lo", 36, 4, F32R)
    ada_raw = temp("ada_raw", 3, 2)
    c_act = temp("condition", 2, 1)
    G = W_AT["mlp1"]

    def act_square_residual(act, r, ready0, done0):
        for k in range(8):
            act.wait_ge(*residual_ready.at(done0 + k + 1))
            act.wait_ge(*square_added.at(ready0 + k - 1))
            nc.scalar.activation(sq[:, k % 2, :], r[:, k, :], ACT.Square).then_inc(square_ready.sem, 1)

    def dve_add_normed(dve, src, r, gain):
        for k in range(8):
            nc.vector.scalar_tensor_tensor(out=src[:, k, :], in0=src[:, k, :], scalar=gain(k),
                                           in1=rstd[:, 0, :], op0=ALU.mult, op1=ALU.mult
                                           ).then_inc(evac.sem, 1)
            dve.wait_ge(*evac.at(k + 1))
            nc.vector.tensor_tensor(r[:, k, :], r[:, k, :], src[:, k, :], ALU.add
                                    ).then_inc(residual_ready.sem, 1)

    with nc.Block() as block:
        def up_block(c):
            return c * 4 + (G - 2)

        def down_block(c):
            return c * 4 + (G + 4)

        @block.sync
        def _(sp):
            sp.wait_ge(*rstd_ready.at(4))

            sp.wait_ge(*tile_tmp.at(8))
            sp.dma_start(c_act[:, 0, :], c_row).then_inc(loaded.sem, 16)

            def load_ada(m0, m):
                sp.wait_ge(*ada_used.at(m0 + (m - 1)))
                sp.dma_start(ada_raw[:, m % 2, :], at_row(wada, m0 + m)).then_inc(ada_landed[m % 2], 16)

            def load_block(b, slot):
                sp.wait_ge(w_split, b * 2 - 2)
                sp.dma_start(w_raw[:, slot, :], at_row(wall, b)).then_inc(w_landed[slot], 16)
            first = G + 3
            load_block(first, first % 2)
            load_block(first + 1, (first + 1) % 2)

            def chunk(c, i, n):
                for q in range(4):
                    load_block(c * 4 + (first + 2 + q), (first + q) % 2)
                    if q < 3:
                        load_ada(i * 6, 3 * n + q)

            def body(i):
                chunk(i * 2, i, 0)
                chunk(i * 2 + 1, i, 1)
            turns(sp, 7, body)
            chunk(14, 7, 0)
            for q in range(3):
                load_ada(42, 3 + q)
            load_block(G + 65, (G + 65) % 2)
            load_block(G + 66, (G + 66) % 2)

        @block.gpsimd
        def _(pool):
            split_weights(pool, G, 64)

        @block.scalar
        def _(act):
            act_rstd(act, 1)
            act_square_residual(act, res, 0, 0)
            act_rstd(act, 2)
            act_apply(act, 8, x_hi, 0)

            def hidden(i, buf, j0, b, n):
                for t in range(2):
                    act.wait_ge(*pair_free.at(j0 + (t + 1)))
                    nc.scalar.activation(tmp[:, t, :], tmp[:, t, :], ACT.Square).then_inc(act_step.sem, 1)
                    act.wait_ge(*act_step.at(n + (t + 1)))
                    nc.scalar.activation(h_hi[:, 2 * buf + t, :], tmp[:, t, :], ACT.Identity
                                         ).then_inc(tile_hi.sem, 1)

            def sum_ada(i, n):
                for q in range(3):
                    m = 3 * n + q
                    act.wait_ge(*ada_full.at(i * 6 + (m + 1)))
                    nc.scalar.activation(ada_raw[:, m % 2, :], ada_raw[:, m % 2, :], ACT.Copy,
                                         accum_out=ada[:, bass.ds(i * 6 + m, 1)]).then_inc(ada_used.sem, 1)
            act.wait_ge(*loaded.at(16))
            nc.scalar.activation(c_act[:, 0, :], c_act[:, 0, :], ACT.Silu).then_inc(ada_read.sem, 1)
            hidden(0, 0, 0, 0, 0)

            def body(i):
                hidden(i, 1, i * 20 + 2, 0, i * 4 + 2)
                sum_ada(i, 0)
                hidden(i, 0, i * 20 + 12, 0, i * 4 + 4)
                sum_ada(i, 1)
            turns(act, 7, body)
            hidden(7, 1, 142, 0, 30)
            sum_ada(7, 0)
            sum_ada(7, 1)

        @block.tensor
        def _(pe):
            pe_stat(pe, 0)
            pe_sum_squares(pe, 8)

            def up(b, j):
                for u in range(2):
                    use_block(pe, b + u, (G + u) % 2, 8, 1, x_hi, x_lo, 0, j + u, u, 2)

            def down(b, j, buf, los):
                pe.wait_ge(*tile_lo.at(los))
                for u in range(2):
                    use_block(pe, b + u, (G + u) % 2, 2, 4, h_hi, h_lo, 2 * buf, j + 4 * u, 0, 2)

            first_two(pe, G, 8, x_hi, x_lo, 0, tile_lo)

            def body(i):
                for n in range(2):
                    up(i * 8 + (G + 2 + 4 * n), i * 20 + (2 + 10 * n))
                    down(i * 8 + (G + 4 + 4 * n), i * 20 + (4 + 10 * n), n, i * 4 + (10 + 2 * n))
            turns(pe, 7, body)
            up(G + 58, 142)
            down(G + 60, 144, 0, 38)
            down(G + 62, 152, 1, 40)

        @block.vector
        def _(dve):
            dve_mean(dve, 1, -1.0 / D)
            dve.wait_ge(*rstd_ready.at(2))
            dve_add_normed(dve, mix, res, lambda k: C1("g_mix_post", k))
            dve_mean(dve, 2, -1.0 / D)
            dve.wait_ge(*rstd_ready.at(4))
            dve_apply(dve, res, 0, 8, lambda k: C1("g_mlp_pre", k), x_lo, x_hi, 0)
            for k in range(8):
                nc.vector.memset(acc[:, k, :], 0.0).then_inc(dve_step.sem, 1)
            dve.wait_ge(*dve_step.at(8))

            def hidden(b, buf, n):
                for t in range(2):
                    wait_tile(dve, b + t, 1, 0, 0)
                    dve.wait_ge(*tile_lo.at(n + (8 + t - 1)))
                    nc.vector.tensor_scalar(tmp[:, t, :], pair(t), 0.0, None, ALU.max
                                            ).then_inc(pair_free.sem, 1)
                    dve.wait_ge(*tile_hi.at(n + (8 + t + 1)))
                    nc.vector.tensor_tensor(h_lo[:, 2 * buf + t, :], tmp[:, t, :],
                                            h_hi[:, 2 * buf + t, :].bitcast(F32), ALU.subtract
                                            ).then_inc(tile_lo.sem, 1)

            def add_down(b, full, a, m0):
                for u in range(2):
                    for m in range(4):
                        wait_tile(dve, b + u, 4, m, full + 3 * u)
                        nc.vector.tensor_tensor(acc[:, 4 * u + m, :], acc[:, 4 * u + m, :], pair(m % 2),
                                                ALU.add).then_inc(pair_free.sem, 1)

            def multiply_ada(i, n):
                for q in range(3):
                    m = 3 * n + q
                    dve.wait_ge(ada_landed[m % 2], i * 48 + 16 * (m // 2 + 1))
                    nc.vector.tensor_tensor(ada_raw[:, m % 2, :], ada_raw[:, m % 2, :], c_act[:, 0, :],
                                            ALU.mult).then_inc(ada_full.sem, 1)
            dve.wait_ge(*ada_read.at(1))
            hidden(G, 0, 0)

            def body(i):
                for n in range(2):
                    hidden(i * 8 + (G + 2 + 4 * n), 1 - n, i * 4 + (2 + 2 * n))
                    add_down(i * 8 + (G + 4 + 4 * n), i * 12 + 6 * n, 0, 0)
                    multiply_ada(i, n)
            turns(dve, 7, body)
            hidden(G + 58, 1, 30)
            add_down(G + 60, 84, 0, 0)
            multiply_ada(7, 0)
            add_down(G + 62, 90, 0, 0)
            multiply_ada(7, 1)
            dve.wait_ge(*ada_used.at(ADA_TILES))
            nc.vector.tensor_tensor(ada[:, :], ada[:, :], ada_bias[:, :], ALU.add).then_inc(ada_read.sem, 1)
    for f, n in ((stat_full, 2), (square_added, 7), (square_ready, 8), (mean_ready, 2), (rstd_ready, 4),
                 (residual_ready, 8), (evac, 8), (tile_tmp, 8), (tile_hi, 40), (tile_lo, 40), (dve_step, 8),
                 (act_step, 32), (pair_free, 160), (tile_full, 96), (ada_used, ADA_TILES),
                 (ada_full, ADA_TILES), (ada_read, 2), (loaded, 16)):
        f.close(n)

    p_raw = slots("p_raw", 32, 2)
    p_hi = slots("p_hi", 34, 2, F32R)
    p_lo = slots("p_lo", 36, 2, F32R)
    emb = acc
    gate = temp("gate", 0, 2)
    sq_res = slots("residual_square", 38, 2)
    GP, GG = W_AT["ple"], W_AT["gate"]
    with nc.Block() as block:
        @block.sync
        def _(sp):
            sp.dma_start(p_raw[:, :, :], p_t).then_inc(loaded.sem, 16)
            load_weights(sp, GP, 10)

        @block.gpsimd
        def _(pool):
            split_weights(pool, GP, 10)

        @block.scalar
        def _(act):
            act_squares(act, acc, 0, 8)
            act.wait_ge(*loaded.at(16))
            for k in range(2):
                nc.scalar.activation(p_hi[:, k, :], p_raw[:, k, :], ACT.Identity).then_inc(tile_hi.sem, 1)
            act_rstd(act, 1)
            for k in range(8):
                act.wait_ge(*residual_ready.at(k + 1))
                nc.scalar.activation(x_hi[:, k, :], res[:, k, :], ACT.Identity).then_inc(tile_hi.sem, 1)
                wait_tile(act, GP + k // 4, 4, k % 4, 3 * (k // 4))
                nc.scalar.activation(emb[:, k, :], pair(k % 2), ACT.Copy).then_inc(emb_ready.sem, 1)
                act.wait_ge(*square_added.at(7 + k - 1))
                nc.scalar.activation(sq[:, k % 2, :], pair(k % 2), ACT.Square).then_inc(pair_free.sem, 1)
            act_rstd(act, 2)
            act.wait_ge(*square_added.at(15))
            for k in range(9):
                if k < 8:
                    wait_tile(act, GG + k, 1, 0, 0)
                    act.wait_ge(*evac.at(8 + k - 1))
                    nc.scalar.activation(gate[:, k % 2, :], pair(k % 2), ACT.Sigmoid).then_inc(act_step.sem, 1)
                if k:
                    act.wait_ge(*pair_free.at(8 + k))
                    act.wait_ge(*square_added.at(15 + k - 2))
                    nc.scalar.activation(sq_res[:, (k - 1) % 2, :], res[:, k - 1, :], ACT.Square
                                         ).then_inc(square_ready.sem, 1)

        @block.tensor
        def _(pe):
            pe_sum_squares(pe, 8)
            pe.wait_ge(*tile_lo.at(2))
            for u in range(2):
                use_block(pe, GP + u, (GP + u) % 2, 2, 4, p_hi, p_lo, 0, 4 * u, 0, 2)
            first_two(pe, GG, 8, x_hi, x_lo, 8, tile_lo, 2)
            pe_stat(pe, 15)
            dense(pe, GG + 2, 6, 8, 1, x_hi, x_lo, job0=10)

        @block.vector
        def _(dve):
            for k in range(2):
                dve.wait_ge(*tile_hi.at(k + 1))
                nc.vector.tensor_tensor(p_lo[:, k, :], p_raw[:, k, :], p_hi[:, k, :].bitcast(F32),
                                        ALU.subtract).then_inc(tile_lo.sem, 1)
            dve_mean(dve, 1, -1.0 / D)
            dve.wait_ge(*rstd_ready.at(2))

            def add_square(k, src, flag, done, added):
                dve.wait_ge(*flag.at(done + k + 1))
                if k:
                    dve.wait_ge(*square_added.at(added + k))
                    nc.vector.tensor_tensor(msq[:, 0, :], msq[:, 0, :], src[:, k % 2, :], ALU.add
                                            ).then_inc(square_added.sem, 1)
                else:
                    nc.vector.tensor_copy(msq[:, 0, :], src[:, 0, :]).then_inc(square_added.sem, 1)

            def low(k):
                dve.wait_ge(*tile_hi.at(3 + k))
                nc.vector.tensor_tensor(x_lo[:, k, :], res[:, k, :], x_hi[:, k, :].bitcast(F32), ALU.subtract
                                        ).then_inc(tile_lo.sem, 1)
            for k in range(8):
                nc.vector.scalar_tensor_tensor(out=acc[:, k, :], in0=acc[:, k, :],
                                               scalar=C1("g_mlp_post", k), in1=rstd[:, 0, :],
                                               op0=ALU.mult, op1=ALU.mult).then_inc(evac.sem, 1)
                dve.wait_ge(*evac.at(k + 1))
                nc.vector.tensor_tensor(res[:, k, :], res[:, k, :], acc[:, k, :], ALU.add
                                        ).then_inc(residual_ready.sem, 1)
                if k:
                    low(k - 1)
                if k >= 2:
                    add_square(k - 2, sq, pair_free, 0, 7)
            low(7)
            add_square(6, sq, pair_free, 0, 7)
            add_square(7, sq, pair_free, 0, 7)
            dve_mean(dve, 2, -1.0 / D)
            dve.wait_ge(*rstd_ready.at(4))
            dve.wait_ge(*emb_ready.at(8))
            for k in range(8):
                nc.vector.scalar_tensor_tensor(out=emb[:, k, :], in0=emb[:, k, :], scalar=C1("g_ple", k),
                                               in1=rstd[:, 0, :], op0=ALU.mult, op1=ALU.mult
                                               ).then_inc(dve_step.sem, 1)
                dve.wait_ge(*act_step.at(k + 1))
                dve.wait_ge(*dve_step.at(k + 1))
                nc.vector.tensor_tensor(emb[:, k, :], emb[:, k, :], gate[:, k % 2, :], ALU.mult
                                        ).then_inc(evac.sem, 1)
                dve.wait_ge(*evac.at(8 + k + 1))
                nc.vector.tensor_tensor(res[:, k, :], res[:, k, :], emb[:, k, :], ALU.add
                                        ).then_inc(pair_free.sem, 1)
                if k:
                    add_square(k - 1, sq_res, square_ready, 8, 15)
            add_square(7, sq_res, square_ready, 8, 15)
    for f, n in ((loaded, 16), (square_ready, 16), (square_added, 23), (stat_full, 2), (mean_ready, 2),
                 (rstd_ready, 4), (tile_hi, 10), (tile_lo, 10), (tile_full, 6), (residual_ready, 8),
                 (evac, 16), (act_step, 8), (dve_step, 8), (emb_ready, 8), (pair_free, 16)):
        f.close(n)

    raw2 = slots("in2_raw", 22, 18)
    CQ, CKV, KRF, FQ, FK, FV = 0, 3, 5, 6, 10, 14
    gate_out = slots("gate_out", 20, 2)
    gain = stat_cols = nc.alloc_sbuf_tensor_at("modulation", [P, 8], F32, offset=SMALL + 5 * 512 - 512)
    G = W_AT["in2"]

    def ada_col(part, k):
        return ada[:, 8 * part + k:8 * part + k + 1]

    def dve_gain(dve, name, part):
        nc.vector.scalar_tensor_tensor(out=gain[:, :], in0=ada[:, 8 * part:8 * part + 8], scalar=1.0,
                                       in1=cols[:, COLS2[name]:COLS2[name] + 8], op0=ALU.add,
                                       op1=ALU.mult).then_inc(dve_step.sem, 1)
        dve.wait_ge(*dve_step.at(1))

    with nc.Block() as block:
        @block.sync
        def _(sp):
            sp.dma_start(cols[:, 0:N_COLS2], cols2).then_inc(loaded.sem, 16)
            sp.dma_start(residual_dram, res[:, :, :]).then_inc(stored.sem, 16)
            load_weights(sp, G, 34)

        @block.gpsimd
        def _(pool):
            split_weights(pool, G, 34)

        @block.scalar
        def _(act):
            act_rstd(act, 1)
            act_apply(act, 8, x_hi, 0, shift=lambda k: ada_col(0, k))
            act.wait_ge(*pair_free.at(18))

            def body(i):
                for u in range(2):
                    wait_tile(act, i * 2 + (G + 18 + u), 1, 0, 0)
                    act.wait_ge(*gate_stored[u].at(i * 16))
                    nc.scalar.activation(gate_out[:, u, :], pair(u), ACT.Sigmoid).then_inc(pair_free.sem, 1)
                    act.wait_ge(*pair_free.at(i * 2 + (18 + u + 1)))
                    act.dma_start(at_row(gates_dram, i * 2 + u), gate_out[:, u, :]).then_inc(gate_stored[u].sem, 16)
            turns(act, 8, body)
            for u in range(2):
                act.wait_ge(*gate_stored[u].at(16 * 8))

        @block.tensor
        def _(pe):
            pe_stat(pe, 0)
            dense(pe, G, 34, 8, 1, x_hi, x_lo, x_flag=tile_lo)

        @block.vector
        def _(dve):
            dve.wait_ge(*loaded.at(16))
            dve_gain(dve, "norm_mix", 1)
            dve_mean(dve, 1, -1.0 / D)
            dve.wait_ge(*rstd_ready.at(2))
            dve_apply(dve, res, 0, 8, lambda k: gain[:, k:k + 1], x_lo, x_hi, 0,
                      shift=lambda k: ada_col(0, k))
            dve.wait_ge(*stored.at(16))

            def body(i):
                for u in range(2):
                    wait_tile(dve, i * 2 + (G + u), 1, 0, 0)
                    nc.vector.tensor_copy(at_tile(raw2, i * 2 + u), pair(u)).then_inc(pair_free.sem, 1)
            turns(dve, 9, body)
    for f, n in ((loaded, 16), (stored, 16), (gate_stored[0], 128), (gate_stored[1], 128),
                 (stat_full, 1),
                 (mean_ready, 1), (rstd_ready, 2), (tile_tmp, 8), (tile_hi, 8), (tile_lo, 8),
                 (dve_step, 1), (pair_free, 34)):
        f.close(n)

    pt_hi = slots("p_turned_hi", 0, 4, F32R, [P, 8, HALF])
    pt_lo = slots("p_turned_lo", 4, 4, F32R, [P, 8, HALF])
    pt0_hi = slots("p_turned_0_hi", 8, 2, F32R, [P, 4, HALF])
    pt0_lo = slots("p_turned_0_lo", 14, 2, F32R, [P, 4, HALF])
    STEPS = 16
    ORDER = (4, 0, 5, 1, 6, 2, 7, 3)

    def block_of(n):
        return ORDER[n % 8]
    GROUPS = [(n, g) for n in range(STEPS) for g in range(block_of(n) // 4 + 1)]
    NG = len(GROUPS)

    def nmax(n):
        return stat[:, 4 * (n % 2):4 * (n % 2) + 1]

    def psum_p(n):
        return stat[:, 4 * (n % 2) + 1:4 * (n % 2) + 2]

    def prsum(n):
        return stat[:, 4 * (n % 2) + 2:4 * (n % 2) + 3]

    def pmax(n):
        return stat[:, 4 * (n % 2) + 3:4 * (n % 2) + 4]

    def turned(q, n):
        return ps[:, 4 + q % 2, 0:n * P].rearrange("q (a b) -> q a b", b=P)

    def first_group(n):
        return sum(1 for m, _ in GROUPS if m < n)

    def turned_out(n):
        return (pt0_hi, pt0_lo) if block_of(n) < 4 else (pt_hi, pt_lo)

    def prob_slot(n):
        return 1 if n == STEPS - 1 else n % STEPS % 3

    def turned_before(n):
        last = [m for m in range(-STEPS, n) if prob_slot(m % STEPS) == prob_slot(n % STEPS)][-1]
        return first_group(last + 1) if last >= 0 else first_group(last + 1 + STEPS) - NG

    def heads_due(p, n):
        k = {-1: (p, 0), 3: (p, 1), 11: (p + 1, 0)}.get(n)
        q = {-1: (p, 0), 7: (p, 1), 15: (p + 1, 0)}.get(n)
        return k, q

    def due(n, wait):
        return [2, 3] if n == STEPS - 1 else [n - 8 - wait] if 0 <= n - 8 - wait < 2 else []

    def softmax_attention(block, scale, prob, vs, act_split, dve_split, pe_ready, operands, o_out, o_tile):
        def steps(lead, now, lag, split, finish, p, last, lag_first):
            for n in range(STEPS):
                more = n + 1 < STEPS or not last
                if n % 8 < 7:
                    if n and lag_first:
                        lag(p, n - 1)
                    split(p, n)
                    lead(p, n + 1)
                    now(p, n)
                    if n and not lag_first:
                        lag(p, n - 1)
                else:
                    now(p, n)
                    if more:
                        split(p, n)
                    lag(p, n - 1)
                    if n + 1 == STEPS:
                        lag(p, n)
                    if more:
                        lead(p, n + 1)
                finish(p, n)

        def pairs(eng, *parts, lag_first=False):
            turns(eng, 3, lambda p: steps(*parts, p, False, lag_first))
            steps(*parts, 3, True, lag_first)

        def nothing(p, n):
            pass

        @block.scalar
        def _(act):
            def exp(p, n):
                w = (block_of(n) + 1) * P
                act.wait_ge(*max_done.at(p * STEPS + (n + 1)))
                if not (isinstance(p, int) and p == 0 and n == 0):
                    act.wait_ge(*turn_full.at(p * NG + max(turned_before(n), 1 - START)))
                nc.scalar.activation(prob[:, prob_slot(n), 0:w], pair(n % 2)[:, 0:w], ACT.Exp, bias=nmax(n),
                                     scale=scale, accum_out=psum_p(n)).then_inc(exp_done.sem, 1)

            def hi(p, n):
                act.wait_ge(*pv_done.at(p * 4 + (2 * (n // 8) - 1 + n % 2)))
                for q, (m, g) in enumerate(GROUPS):
                    if m == n:
                        a, b = 4 * g, min(4 * g + 4, block_of(n) + 1)
                        act.wait_ge(*turn_full.at(p * NG + (q + 1)))
                        nc.scalar.activation(turned_out(n)[0][:, a:b, (block_of(n) % 4) * P:(block_of(n) % 4 + 1) * P],
                                             turned(q, b - a), ACT.Copy).then_inc(tile_hi.sem, 1)

            def output(p, n):
                for k in due(n, 1):
                    act.wait_ge(*pv_done.at(p * 4 + (k + 1)))
                    o_copy(act, p * 4 + k, 1 - k % 2)

            def split(p, n):
                act_split(act, p, n)
            split(0, -1)
            exp(0, 0)
            pairs(act, exp, nothing, hi, split, output, lag_first=True)

        @block.tensor
        def _(pe):
            def scores(p, n):
                i, h = block_of(n), n // 8 % 2
                if n % 8 == 0:
                    pe_ready(pe, p + n // STEPS, h)
                w = (i + 1) * P
                pe.wait_ge(*exp_done.at(p * STEPS + (n - 1)))
                for c in range((w + HALF - 1) // HALF):
                    ks = slice(c * HALF, min(w, (c + 1) * HALF))
                    dst = ps[:, 2 * (n % 2) + c, 0:ks.stop - ks.start]
                    ops = operands(h)
                    for q, (a, b) in enumerate(ops):
                        last = nc.tensor.matmul(dst, a[:, i * P:(i + 1) * P], b[:, ks], start=q == 0,
                                                stop=q == len(ops) - 1)
                        if q == 0 and c == i // 4:
                            nc.tensor.matmul(dst[:, (i % 4) * P:(i % 4 + 1) * P], ident[:, :],
                                             mask[:, :], start=False, stop=False, skip_group_check=True)
                last.then_inc(score_full.sem, 1)

            def turn(p, n):
                pe.wait_ge(*p_ready.at(p * STEPS + (n + 1)))
                for q, (m, g) in enumerate(GROUPS):
                    if m == n:
                        pe.wait_ge(*tile_lo.at(p * NG + (q - 1)))
                        for t in range(4 * g, min(4 * g + 4, block_of(n) + 1)):
                            last = nc.tensor.transpose(ps[:, 4 + q % 2, (t % 4) * P:(t % 4 + 1) * P],
                                                       prob[:, prob_slot(n), t * P:(t + 1) * P], ident_f)
                        last.then_inc(turn_full.sem, 1)

            def values(p, n):
                for k in due(n, 0):
                    h, c = k // 2, 1 - k % 2
                    hi, lo = (pt_hi, pt_lo) if c else (pt0_hi, pt0_lo)
                    if k == 0:
                        pe.wait_ge(*v_split.at(p + 1))
                    pe.wait_ge(*tile_lo.at(p * NG + first_group(8 * h + 7 + k % 2)))
                    pe.wait_ge(*o_free.at(p * 4 + (k - 1)))
                    order = [(0, hi)] + [(j, t) for j in range(1, 4 * c + 4) for t in (hi, lo)]
                    for q, (j, t) in enumerate(order + [(0, lo)]):
                        off = max(0, j - 4 * c) * P
                        last = nc.tensor.matmul(ps[:, 6 + c, off:HALF], vs[:, j, h, :], t[:, j, off:HALF],
                                                start=q == 0, stop=q == len(order), skip_group_check=True)
                    last.then_inc(pv_done.sem, 1)
            scores(0, 0)
            pairs(pe, scores, nothing, turn, nothing, values)

        @block.vector
        def _(dve):
            def top(p, n):
                w = (block_of(n) + 1) * P
                dve.wait_ge(*score_full.at(p * STEPS + (n + 1)))
                nc.vector.tensor_reduce(pmax(n), pair(n % 2)[:, 0:w], AX, ALU.max).then_inc(top_done.sem, 1)
                dve.wait_ge(*top_done.at(p * STEPS + (n + 1)))
                nc.vector.tensor_scalar(nmax(n), pmax(n), -scale, None, ALU.mult).then_inc(max_done.sem, 1)

            def normalise(p, n):
                w = (block_of(n) + 1) * P
                dve.wait_ge(*exp_done.at(p * STEPS + (n + 1)))
                nc.vector.reciprocal(prsum(n), psum_p(n)).then_inc(inverse_done.sem, 1)
                dve.wait_ge(*inverse_done.at(p * STEPS + (n + 1)))
                nc.vector.tensor_scalar(prob[:, prob_slot(n), 0:w], prob[:, prob_slot(n), 0:w], prsum(n), None,
                                        ALU.mult).then_inc(p_ready.sem, 1)

            def lo(p, n):
                hi, low = turned_out(n)
                for q, (m, g) in enumerate(GROUPS):
                    if m == n:
                        a, b = 4 * g, min(4 * g + 4, block_of(n) + 1)
                        dve.wait_ge(*tile_hi.at(p * NG + (q + 1)))
                        cs = slice((block_of(n) % 4) * P, (block_of(n) % 4 + 1) * P)
                        nc.vector.tensor_tensor(low[:, a:b, cs], turned(q, b - a),
                                                hi[:, a:b, cs].bitcast(F32), ALU.subtract
                                                ).then_inc(tile_lo.sem, 1)

            def output(p, n):
                for k in due(n, 1):
                    o_add(dve, p * 4 + k, k // 2, 1 - k % 2, o_out, o_tile(p))

            def split(p, n):
                dve_split(dve, p, n)
            split(0, -1)
            top(0, 0)
            pairs(dve, top, normalise, lo, split, output)

    def close_attention():
        for f, n in ((max_done, STEPS), (exp_done, STEPS), (score_full, STEPS), (p_ready, STEPS),
                     (top_done, STEPS), (inverse_done, STEPS), (turn_full, NG), (tile_hi, NG), (tile_lo, NG), (pv_done, 4),
                     (evac, 4), (o_free, 4)):
            f.close(4 * n)

    v_tok2 = slots("v_tokens_2", 16, 4, F32, [P, 8, HALF])
    fr = slice(HD, HD + 8)
    f_x, f_l, f_cum = (slots(n, k, 1) for n, k in (("forget_x", 0), ("forget_l", 1), ("forget_cum", 2)))
    f_one = slots("forget_ones", 3, 1)
    f_rows = temp("forget_rows", 1, 4, F32R)
    q_both = slots("fox_q_both", 10, 1, F32R, [P, S])
    q_rest = slots("fox_q_rest", 11, 1, F32R, [P, S])
    k_both = [slots(f"fox_k_both_{h}", 12 + h, 1, F32R, [P, S]) for h in range(2)]
    k_rest = [temp("fox_k_rest_0", 0, 1, F32R, [P, S]), slots("fox_k_rest_1", 36, 1, F32R, [P, S])]
    F_ROWS = slice(HD, HD + 4)
    mask_in = slots("mask_in", 8, 1, F32, [P, P])
    with nc.Block() as block:
        @block.sync
        def _(sp):
            sp.dma_start(mask_in[:, :], consts[:, 5 * P:6 * P]).then_inc(loaded.sem, 16)

        @block.scalar
        def _(act):
            load_exp_ln()
            act.wait_ge(*dve_step.at(2))
            nc.scalar.activation(f_l[fr, 0, :], f_x[fr, 0, :], ACT.Abs).then_inc(act_step.sem, 1)
            act.wait_ge(*act_step.at(1))
            nc.scalar.activation(f_l[fr, 0, :], f_l[fr, 0, :], ACT.Exp, scale=-1.0).then_inc(act_step.sem, 1)
            act.wait_ge(*act_step.at(2))
            nc.scalar.activation(f_l[fr, 0, :], f_l[fr, 0, :], ACT.Ln, bias=1.0).then_inc(act_step.sem, 1)

        @block.tensor
        def _(pe):
            for m in range(4):
                if m >= 2:
                    pe.wait_ge(*evac.at(m - 1))
                for b in range(8):
                    last = nc.tensor.transpose(ps[:, 2 * (m % 2) + b // 4, (b % 4) * P:(b % 4 + 1) * P],
                                               raw2[:, FV + m, b * P:(b + 1) * P], ident_f)
                last.then_inc(turn_full.sem, 1)

        @block.vector
        def _(dve):
            n = 0

            def step(ins):
                nonlocal n
                ins.then_inc(dve_step.sem, 1)
                n += 1
                return n
            step(nc.vector.memset(f_one[fr, 0, :], 1.0))
            dve.wait_ge(*dve_step.at(step(nc.vector.tensor_scalar(
                f_x[fr, 0, :], raw2[fr, KRF, :], cols[fr, COLS2["b_forget"]:COLS2["b_forget"] + 1], None,
                ALU.add))))
            step(nc.vector.memset(q_rest[F_ROWS, :].bitcast(F32), 1.0))
            step(nc.vector.memset(k_rest[0][F_ROWS, :].bitcast(F32), 1.0))
            dve.wait_ge(*loaded.at(16))
            step(nc.vector.tensor_copy(mask[:, :], mask_in[:, :]))
            for m in range(4):
                dve.wait_ge(*turn_full.at(m + 1))
                nc.vector.tensor_copy(v_tok2[:, :, m * P:(m + 1) * P],
                                      pair(m % 2).rearrange("p (b n) -> p b n", n=P)
                                      ).then_inc(evac.sem, 1)
            step(nc.vector.memset(k_rest[1][F_ROWS, :].bitcast(F32), 1.0))
            dve.wait_ge(*act_step.at(3))
            dve.wait_ge(*dve_step.at(step(nc.vector.scalar_tensor_tensor(
                out=f_x[fr, 0, :], in0=f_x[fr, 0, :], scalar=0.0, in1=f_l[fr, 0, :], op0=ALU.min,
                op1=ALU.subtract))))
            dve.wait_ge(*dve_step.at(step(nc.vector.tensor_tensor_scan(
                out=f_cum[fr, 0, :], data0=f_one[fr, 0, :], data1=f_x[fr, 0, :], initial=0.0, op0=ALU.mult,
                op1=ALU.add))))
            dve.wait_ge(*dve_step.at(step(nc.vector.tensor_copy(f_rows[fr, 0, :], f_cum[fr, 0, :]))))
            dve.wait_ge(*dve_step.at(step(nc.vector.tensor_tensor(
                f_rows[fr, 1, :], f_cum[fr, 0, :], f_rows[fr, 0, :].bitcast(F32), ALU.subtract))))
            for q in range(2):
                step(nc.vector.tensor_scalar(f_rows[fr, 2 + q, :], f_rows[fr, q, :].bitcast(F32), -1.0, None,
                                             ALU.mult))
            counted.append(n)
    for f, n in ((loaded, 16), (act_step, 3), (turn_full, 4), (evac, 4), (dve_step, counted.pop())):
        f.close(n)

    vs2 = slots("fox_v_split", 20, 2, F32R, [P, 8, 2, P])
    with nc.Block() as block:
        @block.sync
        def _(sp):
            for p in range(4):
                for h in range(2):
                    row = p * 2 + (HD + h)
                    for dst, flag, heads, rows in ((k_rest[h], forget_rows[h], 2, ((0, 2), (1, 3))),
                                                   (q_rest, forget_q, 1, ((2, 0), (3, 1)))):
                        if 2 * p + h >= heads:
                            sp.wait_ge(*score_full.at(p * STEPS + 8 * (h - heads + 1)))
                        for at, src in rows:
                            sp.dma_start(dst[HD + at:HD + at + 1, :].bitcast(F32),
                                         f_rows[row:row + 1, src, :].bitcast(F32)).then_inc(flag.sem, 16)

        def act_split(act, p, n):
            k, q = heads_due(p, n)
            if k is not None and not (isinstance(p, int) and p == 3 and n == 11):
                m, h = k
                if n > 0:
                    act.wait_ge(*score_full.at(m * STEPS + (8 * h - 8)))
                for half in range(2):
                    nc.scalar.activation(k_both[h][half * HD:(half + 1) * HD, :],
                                         at_tile(raw2[h * HD:(h + 1) * HD, :, :], m + FK), ACT.Copy
                                         ).then_inc(k_hi.sem, 1)
            if q is not None:
                m, h = q
                act.wait_ge(*score_full.at(m * STEPS + 8 * h))
                act.wait_ge(*q_split.at(m * 2 + h))
                for dst in (q_both[h * HD:(h + 1) * HD, :], q_rest[0:HD, :]):
                    nc.scalar.activation(dst, at_tile(raw2[h * HD:(h + 1) * HD, :, :], m + FQ), ACT.Copy,
                                         scale=HD ** -0.5).then_inc(q_hi.sem, 1)
            if n == 0:
                act.wait_ge(*pv_done.at(p * 4))
                nc.scalar.activation(vs2[:, :, :, 0:HD], v_pair(v_tok2, p), ACT.Copy).then_inc(v_hi.sem, 1)

        def dve_split(dve, p, n):
            k, q = heads_due(p, n)
            if k is not None and not (isinstance(p, int) and p == 3 and n == 11):
                m, h = k
                dve.wait_ge(*k_hi.at(m * 4 + (2 * h + 2)))
                r = slice(h * HD, (h + 1) * HD)
                nc.vector.tensor_tensor(k_rest[h][0:HD, :], at_tile(raw2[r, :, :], m + FK),
                                        k_both[h][r, :].bitcast(F32), ALU.subtract).then_inc(k_split.sem, 1)
            if q is not None:
                m, h = q
                dve.wait_ge(*q_hi.at(m * 4 + (2 * h + 2)))
                r, other = slice(h * HD, (h + 1) * HD), slice((1 - h) * HD, (2 - h) * HD)
                nc.vector.scalar_tensor_tensor(out=q_both[other, :], in0=at_tile(raw2[r, :, :], m + FQ),
                                               scalar=HD ** -0.5, in1=q_both[r, :].bitcast(F32),
                                               op0=ALU.mult, op1=ALU.subtract).then_inc(q_split.sem, 1)
            if n == 1:
                dve.wait_ge(*v_hi.at(p + 1))
                nc.vector.tensor_tensor(vs2[:, :, :, HD:P], v_pair(v_tok2, p),
                                        vs2[:, :, :, 0:HD].bitcast(F32), ALU.subtract
                                        ).then_inc(v_split.sem, 1)

        def pe_ready(pe, p, h):
            pe.wait_ge(*q_split.at(p * 2 + (h + 1)))
            pe.wait_ge(*k_split.at(p * 2 + (h + 1)))
            pe.wait_ge(*forget_rows[h].at(p * 32 + 32))
            pe.wait_ge(*forget_q.at(p * 64 + (32 * h + 32)))

        def operands(h):
            rows = slice(0, HD + 4)
            return (q_both, k_both[h]), (q_rest[rows, :], k_rest[h][rows, :])
        softmax_attention(block, 1.0, slots("prob_fox", 37, 3), vs2, act_split, dve_split, pe_ready, operands, raw2,
                          lambda p: p + FQ)
    close_attention()
    for f, n in ((q_split, 8), (k_split, 8), (q_hi, 16), (k_hi, 16), (v_hi, 4), (v_split, 4),
                 (forget_rows[0], 128), (forget_rows[1], 128), (forget_q, 256)):
        f.close(n)

    cx_hi = slots("latent_hi", 0, 5, F32R)
    cx_lo = slots("latent_lo", 5, 5, F32R)
    qm = slots("mla_q", 32, 8)
    km = slots("mla_k", 16, 4)
    vt = slots("mla_v", 10, 4)
    v_tok3 = slots("v_tokens_3", 20, 4, F32, [P, 8, HALF])
    rope_cos = slots("rope_cos", 14, 1)
    rope_sin = slots("rope_sin", 15, 1)
    pos_in = temp("positions", 0, 1, I32)
    r_a, r_b, r_c = temp("rope_a", 0, 1), temp("rope_b", 1, 1), temp("rope_c", 4, 1)
    TWO_PI = 6.283185307179586
    PI_PARTS = (6.28125, 0.0019350051879882812, 3.0199159819e-07)
    ROUND = 12582912.0
    with nc.Block() as block:
        @block.sync
        def _(sp):
            sp.dma_start(pos_in[:, 0, :], pos).then_inc(loaded.sem, 16)

        @block.scalar
        def _(act):
            for q in range(2):
                act.wait_ge(*dve_step.at(counts[q]))
                nc.scalar.activation((rope_sin, rope_cos)[q][:, 0, :], (rope_sin, rope_cos)[q][:, 0, :],
                                     ACT.Sin).then_inc(act_step.sem, 1)

        @block.vector
        def _(dve):
            n = 0
            dve.wait_ge(*loaded.at(16))

            def step(ins):
                nonlocal n
                ins.then_inc(dve_step.sem, 1)
                n += 1
                dve.wait_ge(*dve_step.at(n))
            V = nc.vector
            step(V.tensor_copy(r_b[:, 0, :], pos_in[:, 0, :]))
            step(V.tensor_scalar(r_b[:, 0, :], r_b[:, 0, :], C2("inv_freq", 0), None, ALU.mult))
            for q, (dst, turn) in enumerate(((rope_sin, 0.0), (rope_cos, 0.25))):
                step(V.tensor_scalar(r_c[:, 0, :], r_b[:, 0, :], 1.0 / TWO_PI, turn, ALU.mult, ALU.add))
                step(V.tensor_scalar(r_c[:, 0, :], r_c[:, 0, :], ROUND, None, ALU.add))
                step(V.tensor_scalar(r_c[:, 0, :], r_c[:, 0, :], ROUND, None, ALU.subtract))
                for i, part in enumerate(PI_PARTS):
                    step(V.scalar_tensor_tensor(out=dst[:, 0, :], in0=r_c[:, 0, :], scalar=-part,
                                                in1=(dst if i else r_b)[:, 0, :], op0=ALU.mult, op1=ALU.add))
                step(V.tensor_scalar(dst[:, 0, :], dst[:, 0, :], turn * TWO_PI, 3.141592, ALU.add, ALU.min))
                step(V.tensor_scalar(dst[:, 0, :], dst[:, 0, :], -3.141592, None, ALU.max))
                assert n == counts[q]
    for f, n in ((loaded, 16), (act_step, 2), (dve_step, counts[1])):
        f.close(n)

    GQ, GK = W_AT["uq"], W_AT["ukv"]
    with nc.Block() as block:
        @block.sync
        def _(sp):
            load_weights(sp, GQ, 6)

        @block.gpsimd
        def _(pool):
            split_weights(pool, GQ, 6)

        @block.scalar
        def _(act):
            act_squares(act, raw2, CQ, 3)
            act_rstd(act, 1)
            act_apply(act, 3, cx_hi, 0)
            act.wait_ge(*tile_lo.at(3))
            for k in range(2):
                nc.scalar.activation(sq[:, k, :], raw2[:, CKV + k, :], ACT.Square).then_inc(square_ready.sem, 1)
            act_rstd(act, 2)
            act_apply(act, 2, cx_hi, 3, done=3)
            for h in range(8):
                wait_tile(act, GQ + h // 2, 2, h % 2, h // 2)
                nc.scalar.activation(qm[0:HD, h, :], pair(h % 2)[0:HD, :], ACT.Copy).then_inc(act_step.sem, 1)

        @block.tensor
        def _(pe):
            pe_stat(pe, 3)
            pe_stat(pe, 5)
            dense(pe, GQ, 4, 3, 2, cx_hi, cx_lo, x_flag=tile_lo)
            pe.wait_ge(*tile_lo.at(5))
            for u in range(2):
                use_block(pe, GK + u, (GK + u) % 2, 2, 4, cx_hi, cx_lo, 3, 8 + 4 * u, 0, 2)
            for m in range(4):
                pe.wait_ge(*pair_free.at(16 + m - 1))
                for b in range(8):
                    last = nc.tensor.transpose(ps[:, 2 * (m % 2) + b // 4, (b % 4) * P:(b % 4 + 1) * P],
                                               vt[:, m, b * P:(b + 1) * P], ident_f)
                last.then_inc(turn_full.sem, 1)

        @block.vector
        def _(dve):
            dve_sum_squares(dve, 3)
            dve_mean(dve, 1, -1.0 / 384)
            dve.wait_ge(*rstd_ready.at(2))
            dve_apply(dve, raw2, CQ, 3, lambda k: C2("q_norm", k), cx_lo, cx_hi, 0)
            dve_sum_squares(dve, 2, 3, 3)
            dve_mean(dve, 2, -1.0 / 256)
            dve.wait_ge(*rstd_ready.at(4))
            dve_apply(dve, raw2, CKV, 2, lambda k: C2("kv_norm", k), cx_lo, cx_hi, 3, done=3)
            rows, swap = slice(HD, HD + ROPE), slice(HD + ROPE, P)
            dve.wait_ge(*tile_lo.at(5))
            for h in range(8):
                wait_tile(dve, GQ + h // 2, 2, h % 2, h // 2)
                nc.vector.tensor_tensor(qm[rows, h, :], pair(h % 2)[rows, :], rope_cos[rows, 0, :], ALU.mult
                                        ).then_inc(dve_step.sem, 1)
                dve.wait_ge(*act_step.at(h + 1))
                if h >= 1:
                    dve.wait_ge(*dve_step.at(2 * h))
                nc.vector.tensor_tensor(r_a[rows, 0, :], pair(h % 2)[swap, :], rope_sin[swap, 0, :], ALU.mult
                                        ).then_inc(pair_free.sem, 1)
                dve.wait_ge(*pair_free.at(h + 1))
                dve.wait_ge(*dve_step.at(2 * h + 1))
                nc.vector.tensor_tensor(qm[rows, h, :], qm[rows, h, :], r_a[rows, 0, :], ALU.add
                                        ).then_inc(dve_step.sem, 1)
            for u in range(2):
                for m in range(4):
                    wait_tile(dve, GK + u, 4, m, 4 + 3 * u)
                    nc.vector.tensor_copy((km, vt)[u][:, m, :], pair(m % 2)).then_inc(pair_free.sem, 1)
            for m in range(4):
                dve.wait_ge(*turn_full.at(m + 1))
                nc.vector.tensor_copy(v_tok3[:, :, m * P:(m + 1) * P],
                                      pair(m % 2).rearrange("p (b n) -> p b n", n=P)
                                      ).then_inc(pair_free.sem, 1)
    for f, n in ((square_ready, 5), (square_added, 5), (stat_full, 2), (mean_ready, 2), (rstd_ready, 4),
                 (tile_tmp, 5), (tile_hi, 5), (tile_lo, 5), (act_step, 8), (dve_step, 16), (turn_full, 4),
                 (tile_full, 4 + 6), (pair_free, 20)):
        f.close(n)

    m_qh = slots("mla_q_hi", 10, 1, F32R)
    m_ql = slots("mla_q_lo", 11, 1, F32R)
    m_kh = [slots("mla_k_hi_0", 12, 1, F32R), slots("mla_k_hi_1", 26, 1, F32R)]
    m_kl = [slots("mla_k_lo_0", 13, 1, F32R), slots("mla_k_lo_1", 27, 1, F32R)]
    k_in = temp("mla_k_in", 0, 1)
    r_k = temp("rope_k", 1, 1)
    vs3 = slots("mla_v_split", 28 - 4, 2, F32R, [P, 8, 2, P])
    E_ROWS = slice(0, NOPE + ROPE)
    with nc.Block() as block:
        @block.scalar
        def _(act):
            act.wait_ge(*dve_step.at(3))
            for h in range(2):
                nc.scalar.activation(m_kh[h][HD:HD + ROPE, 0, :], r_k[HD:HD + ROPE, 0, :], ACT.Identity
                                     ).then_inc(act_step.sem, 1)

        @block.vector
        def _(dve):
            rows = slice(HD, HD + ROPE)
            nc.vector.tensor_tensor(r_k[rows, 0, :], raw2[0:ROPE, KRF, :], rope_cos[0:ROPE, 0, :], ALU.mult
                                    ).then_inc(dve_step.sem, 1)
            nc.vector.tensor_tensor(k_in[rows, 0, :], raw2[ROPE:2 * ROPE, KRF, :], rope_sin[ROPE:2 * ROPE, 0, :],
                                    ALU.mult).then_inc(dve_step.sem, 1)
            dve.wait_ge(*dve_step.at(2))
            nc.vector.tensor_tensor(r_k[rows, 0, :], r_k[rows, 0, :], k_in[rows, 0, :], ALU.add
                                    ).then_inc(dve_step.sem, 1)
            for h in range(2):
                dve.wait_ge(*act_step.at(h + 1))
                nc.vector.tensor_tensor(m_kl[h][rows, 0, :], r_k[rows, 0, :], m_kh[h][rows, 0, :].bitcast(F32),
                                        ALU.subtract).then_inc(dve_step.sem, 1)
    act_step.close(2)
    dve_step.close(5)
    with nc.Block() as block:
        def act_split3(act, p, n):
            k, q = heads_due(p, n)
            if k is not None and not (isinstance(p, int) and p == 3 and n == 11):
                m, h = k
                act.wait_ge(*k_split.at(m * 2 + h))
                if n > 0:
                    act.wait_ge(*score_full.at(m * STEPS + (8 * h - 8)))
                nc.scalar.activation(k_in[0:HD, 0, :], at_tile(km[h * HD:(h + 1) * HD, :, :], m), ACT.Copy
                                     ).then_inc(k_in_ready.sem, 1)
                act.wait_ge(*k_in_ready.at(m * 2 + (h + 1)))
                nc.scalar.activation(m_kh[h][0:HD, 0, :], k_in[0:HD, 0, :], ACT.Copy).then_inc(k_hi.sem, 1)
            if q is not None:
                m, h = q
                act.wait_ge(*score_full.at(m * STEPS + 8 * h))
                act.wait_ge(*q_split.at(m * 2 + h))
                nc.scalar.activation(m_qh[E_ROWS, 0, :], at_tile(qm[E_ROWS, :, :], m * 2 + h), ACT.Copy
                                     ).then_inc(q_hi.sem, 1)
            if n == 0:
                act.wait_ge(*pv_done.at(p * 4))
                nc.scalar.activation(vs3[:, :, :, 0:HD], v_pair(v_tok3, p), ACT.Copy).then_inc(v_hi.sem, 1)

        def dve_split3(dve, p, n):
            k, q = heads_due(p, n)
            if k is not None and not (isinstance(p, int) and p == 3 and n == 11):
                m, h = k
                dve.wait_ge(*k_hi.at(m * 2 + (h + 1)))
                nc.vector.tensor_tensor(m_kl[h][0:HD, 0, :], k_in[0:HD, 0, :],
                                        m_kh[h][0:HD, 0, :].bitcast(F32), ALU.subtract).then_inc(k_split.sem, 1)
            if q is not None:
                m, h = q
                dve.wait_ge(*q_hi.at(m * 2 + (h + 1)))
                nc.vector.tensor_tensor(m_ql[E_ROWS, 0, :], at_tile(qm[E_ROWS, :, :], m * 2 + h),
                                        m_qh[E_ROWS, 0, :].bitcast(F32), ALU.subtract).then_inc(q_split.sem, 1)
            if n == 1:
                dve.wait_ge(*v_hi.at(p + 1))
                nc.vector.tensor_tensor(vs3[:, :, :, HD:P], v_pair(v_tok3, p),
                                        vs3[:, :, :, 0:HD].bitcast(F32), ALU.subtract
                                        ).then_inc(v_split.sem, 1)

        def pe_ready3(pe, p, h):
            pe.wait_ge(*q_split.at(p * 2 + (h + 1)))
            pe.wait_ge(*k_split.at(p * 2 + (h + 1)))

        def operands3(h):
            return tuple((a[E_ROWS, 0, :], b[E_ROWS, 0, :])
                         for a, b in ((m_qh, m_kh[h]), (m_qh, m_kl[h]), (m_ql, m_kh[h])))
        softmax_attention(block, MLA_SCALE, temp("prob_mla", 1, 3), vs3, act_split3, dve_split3, pe_ready3, operands3, qm,
                          lambda p: p * 2)
    close_attention()
    for f, n in ((k_in_ready, 8), (k_hi, 8), (k_split, 8), (q_hi, 8), (q_split, 8), (v_hi, 4), (v_split, 4)):
        f.close(n)

    om_hi, om_lo = slots("o_mla_hi", 0, 4, F32R), slots("o_mla_lo", 4, 4, F32R)
    of_hi, of_lo = slots("o_fox_hi", 8, 4, F32R), slots("o_fox_lo", 12, 4, F32R)
    y2_hi, y2_lo = slots("y2_hi", 16, 8, F32R), slots("y2_lo", 24, 8, F32R)
    g_in = slots("gate_in", 32, 8)
    y_t = temp("gated", 0, 4)
    G = W_AT["o2"]

    def load_gates(eng, i):
        for q in range(2):
            at = 4 * (i % 2) + 2 * q
            eng.dma_start(g_in[:, at:at + 2, :], gates_dram[8 * q + 2 * i:8 * q + 2 * i + 2, :, :]
                          .rearrange("m p n -> p m n")).then_inc(gates_in[i % 2].sem, 16)
    with nc.Block() as block:
        @block.sync
        def _(sp):
            sp.wait_ge(*tile_lo.at(4))
            for i in range(2):
                load_gates(sp, i)
            load_weights(sp, G, 8)

        @block.gpsimd
        def _(pool):
            split_weights(pool, G, 8)

        @block.scalar
        def _(act):
            for k in range(4):
                nc.scalar.activation(om_hi[:, k, :], qm[:, 2 * k, :], ACT.Identity).then_inc(tile_hi.sem, 1)
            for k in range(4):
                nc.scalar.activation(of_hi[:, k, :], raw2[:, FQ + k, :], ACT.Identity).then_inc(tile_hi.sem, 1)
            for m in range(8):
                act.wait_ge(*tile_tmp.at(m + 1))
                nc.scalar.activation(y2_hi[:, m, :], y_t[:, m % 2, :], ACT.Identity).then_inc(tile_hi.sem, 1)
                if m in (1, 3):
                    load_gates(act, 2 + m // 2)

        @block.tensor
        def _(pe):
            pe.wait_ge(*tile_lo.at(8))
            for i in range(4):
                for q, (a, b) in enumerate(((om_hi, om_lo), (of_hi, of_lo))):
                    use_block(pe, G + 2 * i + q, (G + q) % 2, 4, 2, a, b, 0, 4 * i + 2 * q, 2 * q, 4)

        @block.vector
        def _(dve):
            for k in range(8):
                dve.wait_ge(*tile_hi.at(k + 1))
                src, hi, lo = ((qm[:, 2 * k, :], om_hi, om_lo) if k < 4 else
                               (raw2[:, FQ + k - 4, :], of_hi, of_lo))
                nc.vector.tensor_tensor(lo[:, k % 4, :], src, hi[:, k % 4, :].bitcast(F32), ALU.subtract
                                        ).then_inc(tile_lo.sem, 1)
            for i in range(4):
                for q in range(2):
                    for m in range(2):
                        wait_tile(dve, G + 2 * i + q, 2, m, 2 * i + q)
                        dve.wait_ge(*gates_in[i % 2].at(32 * (i // 2) + 32))
                        if q == 0:
                            dve.wait_ge(*tile_lo.at(8 + 2 * i - 2 + m + 1))
                        nc.vector.tensor_tensor(y_t[:, 2 * q + m, :], pair(2 * q + m),
                                                g_in[:, 4 * (i % 2) + 2 * q + m, :], ALU.mult
                                                ).then_inc(pair_free.sem, 1)
                for m in range(2):
                    dve.wait_ge(*pair_free.at(4 * i + 4))
                    nc.vector.tensor_tensor(y_t[:, m, :], y_t[:, m, :], y_t[:, 2 + m, :], ALU.add
                                            ).then_inc(tile_tmp.sem, 1)
                    dve.wait_ge(*tile_hi.at(8 + 2 * i + m + 1))
                    nc.vector.tensor_tensor(y2_lo[:, 2 * i + m, :], y_t[:, m, :],
                                            y2_hi[:, 2 * i + m, :].bitcast(F32), ALU.subtract
                                            ).then_inc(tile_lo.sem, 1)
    for f, n in ((gates_in[0], 64), (gates_in[1], 64), (tile_hi, 16), (tile_lo, 16), (tile_tmp, 8), (tile_full, 8), (pair_free, 16)):
        f.close(n)

    res2 = slots("residual_2", 0, 8)
    G = W_AT["out2"]
    with nc.Block() as block:
        @block.sync
        def _(sp):
            sp.dma_start(res2[:, :, :], residual_dram).then_inc(loaded.sem, 16)
            load_weights(sp, G, 8)
            sp.wait_ge(*loaded.at(16))

        @block.gpsimd
        def _(pool):
            split_weights(pool, G, 8)

        @block.tensor
        def _(pe):
            dense(pe, G, 8, 8, 1, y2_hi, y2_lo)

        @block.scalar
        def _(act):
            for k in range(8):
                act.wait_ge(*pair_free.at(k + 1))
                if k >= 2:
                    act.wait_ge(*square_added.at(k - 1))
                nc.scalar.activation(sq[:, k % 2, :], res2[:, k, :], ACT.Square).then_inc(square_ready.sem, 1)

        @block.vector
        def _(dve):
            def add_square(k):
                dve.wait_ge(*square_ready.at(k + 1))
                if k:
                    dve.wait_ge(*square_added.at(k))
                    nc.vector.tensor_tensor(msq[:, 0, :], msq[:, 0, :], sq[:, k % 2, :], ALU.add
                                            ).then_inc(square_added.sem, 1)
                else:
                    nc.vector.tensor_copy(msq[:, 0, :], sq[:, 0, :]).then_inc(square_added.sem, 1)
            dve.wait_ge(*loaded.at(16))
            for k in range(8):
                wait_tile(dve, G + k, 1, 0, 0)
                nc.vector.scalar_tensor_tensor(out=res2[:, k, :], in0=pair(k % 2), scalar=ada_col(2, k),
                                               in1=res2[:, k, :], op0=ALU.mult, op1=ALU.add
                                               ).then_inc(pair_free.sem, 1)
                if k:
                    add_square(k - 1)
            add_square(7)
    for f, n in ((loaded, 16), (pair_free, 8), (square_ready, 8), (square_added, 8)):
        f.close(n)

    x2_hi, x2_lo = y2_hi, y2_lo
    acc2 = slots("accumulator_2", 8, 8)
    h2_hi = slots("hidden2_hi", 32, 4, F32R)
    h2_lo = slots("hidden2_lo", 36, 4, F32R)
    G = W_AT["mlp2"]
    norm_counts = ((stat_full, 1), (mean_ready, 1), (rstd_ready, 2), (tile_tmp, 8), (tile_hi, 8),
                   (tile_lo, 8), (dve_step, 1))

    conv_y = temp("conv_out", 0, 3)
    with nc.Block() as block:
        @block.sync
        def _(sp):
            load_weights(sp, G, 66)

        @block.gpsimd
        def _(pool):
            split_weights(pool, G, 66)

        def conv_col(name, half, tile):
            return tile + COLS2[name] + 22 * half

        def jobs(n, t):
            if isinstance(n, int) and n == 0:
                return 2 * t + 2
            return n * 6 + (2 * t + 2 - 8)

        def pair_free_up(n, t, half):
            return dve_step.at(n * 2 + (2 * t + half + 1))

        def chunks(eng, up, down, _):
            up((G, 0, 0, 0), 0)

            def body(i):
                for n in range(2):
                    up((i * 12 + (G + 4 + 6 * n), 1 - n, i * 4 + (2 + 2 * n), i * 4 + (2 + 2 * n)), 0)
                    if down:
                        down(i, n)
            turns(eng, 5, body)
            if down:
                down(5, 0)

        def at_col(c):
            return cols[:, c:c + 1] if isinstance(c, int) else cols[:, bass.ds(c, 1)]

        @block.scalar
        def _(act):
            act_rstd(act, 1)
            act_apply(act, 8, x2_hi, 0, shift=lambda k: ada_col(3, k))

            def hidden(b, buf, tile0, n):
                for t in range(2):
                    for half in range(2):
                        wait_tile(act, b + 2 * t + half, 1, 0, 0)
                        act.wait_ge(*tile_lo.at(n + t))
                        nc.scalar.activation(conv_y[:, half, :], pair(half), ACT.Identity,
                                             scale=at_col(tile0 + (t + conv_col("conv2", half, 0))),
                                             bias=at_col(tile0 + (t + conv_col("conv_b", half, 0)))
                                             ).then_inc(evac.sem, 1)
                    act.wait_ge(*pair_free.at(jobs(n, t) - 1))
                    nc.scalar.activation(conv_y[:, 2, :], conv_y[:, 0, :], ACT.Silu).then_inc(act_step.sem, 1)
                    act.wait_ge(*tile_tmp.at(n + (t + 1)))
                    nc.scalar.activation(h2_hi[:, 2 * buf + t, :], conv_y[:, 1, :], ACT.Identity
                                         ).then_inc(tile_hi.sem, 1)
            with after(norm_counts):
                act.wait_ge(*tile_lo.at(0))
                chunks(act, lambda c, n: hidden(*c), None, None)

        @block.tensor
        def _(pe):
            def up(b, j):
                for u in range(4):
                    use_block(pe, b + u, (G + u) % 2, 8, 1, x2_hi, x2_lo, 0, j + u, u, 2)

            def down(b, j, buf, los):
                pe.wait_ge(*tile_lo.at(8 + los))
                for u in range(2):
                    use_block(pe, b + u, (G + u) % 2, 2, 4, h2_hi, h2_lo, 2 * buf, j + 4 * u, 0, 2)
            pe_stat(pe, 0)
            first_two(pe, G, 8, x2_hi, x2_lo, 0, tile_lo)
            for u in range(2, 4):
                use_block(pe, G + u, (G + u) % 2, 8, 1, x2_hi, x2_lo, 0, u, u, 2)

            def body(i):
                for n in range(2):
                    up(i * 12 + (G + 4 + 6 * n), i * 24 + (4 + 12 * n))
                    down(i * 12 + (G + 8 + 6 * n), i * 24 + (8 + 12 * n), n, i * 4 + (2 + 2 * n))
            turns(pe, 5, body)
            down(G + 64, 124, 0, 22)

        @block.vector
        def _(dve):
            dve_gain(dve, "norm_ffn", 4)
            dve_mean(dve, 1, -1.0 / D)
            dve.wait_ge(*rstd_ready.at(2))
            dve_apply(dve, res2, 0, 8, lambda k: gain[:, k:k + 1], x2_lo, x2_hi, 0,
                      shift=lambda k: ada_col(3, k))
            for k in range(8):
                nc.vector.memset(acc2[:, k, :], 0.0).then_inc(acc_zero.sem, 1)
            dve.wait_ge(*acc_zero.at(8))

            def hidden(b, buf, tile0, n):
                for t in range(2):
                    for half in range(2):
                        dve.wait_ge(*evac.at(n * 2 + (2 * t + half + 1)))
                        y, z = conv_y[:, half, :], pair(half)
                        nc.vector.scalar_tensor_tensor(
                            out=y[:, 1:S], in0=z[:, 0:S - 1],
                            scalar=at_col(tile0 + (t + conv_col("conv1", half, 0))), in1=y[:, 1:S],
                            op0=ALU.mult, op1=ALU.add).then_inc(dve_step.sem, 1)
                        dve.wait_ge(*pair_free_up(n, t, half))
                        nc.vector.scalar_tensor_tensor(
                            out=y[:, 2:S], in0=z[:, 0:S - 2],
                            scalar=at_col(tile0 + (t + conv_col("conv0", half, 0))), in1=y[:, 2:S],
                            op0=ALU.mult, op1=ALU.add).then_inc(pair_free.sem, 1)
                    dve.wait_ge(*act_step.at(n + (t + 1)))
                    dve.wait_ge(*pair_free.at(jobs(n, t)))
                    nc.vector.tensor_tensor(conv_y[:, 1, :], conv_y[:, 1, :], conv_y[:, 2, :], ALU.mult
                                            ).then_inc(tile_tmp.sem, 1)
                    dve.wait_ge(*tile_hi.at(n + (t + 1)))
                    nc.vector.tensor_tensor(h2_lo[:, 2 * buf + t, :], conv_y[:, 1, :],
                                            h2_hi[:, 2 * buf + t, :].bitcast(F32), ALU.subtract
                                            ).then_inc(tile_lo.sem, 1)

            def down(i, n):
                b = i * 12 + (G + 8 + 6 * n) if not isinstance(i, int) else G + 64
                for u in range(2):
                    for m in range(4):
                        wait_tile(dve, b + u, 4, m, i * 12 + (6 * n + 3 * u))
                        nc.vector.tensor_tensor(acc2[:, 4 * u + m, :], acc2[:, 4 * u + m, :], pair(m % 2),
                                                ALU.add).then_inc(pair_free.sem, 1)
            with after(norm_counts):
                chunks(dve, lambda c, n: hidden(*c), down, None)
    for f, n in ((evac, 44), (dve_step, 44), (pair_free, 132), (act_step, 22), (tile_tmp, 22), (tile_hi, 22),
                 (tile_lo, 22), (tile_full, 66), (acc_zero, 8), *norm_counts):
        f.close(n)

    final = x2_out = slots("final", 16, 8)
    with nc.Block() as block:
        @block.scalar
        def _(act):
            act_square_residual(act, res2, 0, 0)
            act_rstd(act, 1)

        @block.tensor
        def _(pe):
            pe_sum_squares(pe, 8)

        @block.vector
        def _(dve):
            for k in range(8):
                nc.vector.scalar_tensor_tensor(out=res2[:, k, :], in0=acc2[:, k, :], scalar=ada_col(5, k),
                                               in1=res2[:, k, :], op0=ALU.mult, op1=ALU.add
                                               ).then_inc(residual_ready.sem, 1)
            dve_mean(dve, 1, -1.0 / D)
            dve.wait_ge(*rstd_ready.at(2))
            for k in range(8):
                nc.vector.scalar_tensor_tensor(out=final[:, k, :], in0=res2[:, k, :],
                                               scalar=C2("norm_final", k), in1=rstd[:, 0, :],
                                               op0=ALU.mult, op1=ALU.mult).then_inc(tile_tmp.sem, 1)

        @block.sync
        def _(sp):
            for k in range(8):
                sp.wait_ge(*tile_tmp.at(k + 1))
                sp.dma_start(out[:, k, :], final[:, k, :]).then_inc(stored.sem, 16)
            sp.wait_ge(*stored.at(128))


def kernel(**inputs):
    import numpy as np
    import concourse.bacc as _bacc
    from concourse.bass_utils import run_bass_kernel_spmd as _run

    a = {k: np.asarray(v) for k, v in inputs.items()}
    f32 = np.float32

    def tiles(w, kt):
        k, n = w.shape
        return w.reshape(k // P, P, n // P, P).transpose(2, 0, 1, 3)

    def blocks(t, per):
        m, kt = t.shape[:2]
        out = np.zeros((m // per, P, KD, P), f32)
        out[:, :, :per * kt, :] = t.reshape(m // per, per * kt, P, P).transpose(0, 2, 1, 3)
        return out.reshape(m // per, P, S)

    def strips(w):
        return blocks(tiles(w, w.shape[0] // P), KD // (w.shape[0] // P))

    w_in = a["w_in"][0]
    parts = [strips(np.concatenate([w_in[:, 512:], w_in[:, :512]], 1))]
    pool = np.zeros((1, P, KD, P), f32)
    pool[0, :, :4, :] = a["w_pool"][0].transpose(1, 0, 2)
    parts.append(pool.reshape(1, P, S))
    parts.append(strips(a["w_out"][0]))

    def interleave(up, down, per_up):
        n = len(down) // 2
        out = [up[:per_up]]
        for c in range(n):
            out.append(up[(c + 1) * per_up:(c + 2) * per_up])
            out.append(down[2 * c:2 * c + 2])
        return np.concatenate(out)

    def down_blocks(w):
        n = w.shape[0] // 256
        return np.concatenate([strips(w[256 * c:256 * c + 256]) for c in range(n)])
    parts.append(interleave(strips(a["w_up"][0]), down_blocks(a["w_down"][0]), 2))
    parts.append(strips(a["w_ple_proj"][0]))
    parts.append(strips(a["w_ple_gate"][0]))
    w2 = a["w_in_2"][0]
    cut = np.cumsum([0, 384, 256, 32, 512, 512, 512, 8, 1024, 1024])
    cq, ckv, kr, fq, fk, fv, fl, gm, gf = (w2[:, cut[i]:cut[i + 1]] for i in range(9))
    swap = np.concatenate([np.arange(16, 32), np.arange(16)])
    krf = np.concatenate([kr, kr[:, swap], fl, np.zeros((D, 56), f32)], 1)
    parts.append(strips(np.concatenate([cq, ckv, krf, fq, fk, fv, gm, gf], 1)))
    uq = a["w_uq_2"][0].reshape(384, 8, 96)
    uq = np.concatenate([uq, uq[:, :, 64 + swap]], 2).reshape(384, 1024)
    parts.append(strips(uq))
    ukv = a["w_ukv_2"][0].reshape(256, 8, 2, 64).transpose(0, 2, 1, 3).reshape(256, 1024)
    parts.append(strips(ukv))
    om, of = strips(a["w_o_mla_2"][0]), strips(a["w_o_fox_2"][0])
    parts.append(np.stack([om, of], 1).reshape(8, P, S))
    parts.append(strips(a["w_out_2"][0]))
    up2 = strips(a["w_up_2"][0]).reshape(2, 22, P, S).transpose(1, 0, 2, 3).reshape(44, P, S)
    parts.append(interleave(up2, down_blocks(a["w_down_2"][0]), 4))
    wall = np.concatenate(parts)
    wada = a["w_ada_2"][0].T.reshape(ADA_TILES, P, D)

    def column(v):
        return np.asarray(v, f32).reshape(-1, P).T

    cols1 = np.concatenate([column(a[n].ravel()) for n in (
        "g_mix_pre", "pool_scale", "g_sb", "g_mix_post", "g_mlp_pre", "g_mlp_post", "g_ple")], 1)
    bf = np.zeros((P, 1), f32)
    bf[64:72, 0] = a["b_forget_2"][0]
    half = (10000.0 ** (-np.arange(0, 32, 2, dtype=f32) / f32(32))).astype(f32)
    inv = np.tile(np.concatenate([-half, half]), 4).reshape(P, 1).astype(f32)
    cw = a["conv_w_2"][0]
    cols2 = np.concatenate([column(a[n].ravel()) for n in (
        "norm_mix_g_2", "q_norm_g_2", "kv_norm_g_2", "norm_ffn_g_2", "norm_final_g_2")]
        + [bf, inv, column(cw[0]), column(cw[1]), column(cw[2]), column(a["conv_b_2"][0])], 1)
    b_ada = column(a["b_ada_2"][0])
    i = np.arange(P)
    consts = np.concatenate([
        np.eye(P), -np.ones((P, P)), -(i[:, None] >= i[None, :]).astype(f32),
        np.where(i[:, None] < i[None, :], 0.0, NEG),
        (i[:, None] // 64 == i[None, :] // 64).astype(f32),
        np.where(i[None, :] <= i[:, None], 0.0, NEG),
        np.tile(1.0 / np.arange(1, 17), (P, 1))], 1).astype(f32)
    x_t = a["x"][0].T.reshape(KD, P, S).transpose(1, 0, 2)
    p_t = a["p"][0, 0].T.reshape(2, P, S).transpose(1, 0, 2)
    c_row = np.broadcast_to(a["c_2"], (P, D))
    pos = np.broadcast_to(a["positions_2"], (P, S))

    nc = _bacc.Bacc("TRN2", target_bir_lowering=False, num_devices=1)
    arrays, args = {}, []
    for name, v, dt in (("wall", wall, F32), ("wada", wada, F32), ("x_t", x_t, F32), ("p_t", p_t, F32), ("c_row", c_row, F32),
                        ("cols1", cols1, F32), ("cols2", cols2, F32), ("b_ada", b_ada, F32),
                        ("pos", pos, I32), ("consts", consts, F32)):
        arrays[name] = np.ascontiguousarray(v)
        args.append(nc.dram_tensor(name, arrays[name].shape, dt, kind="ExternalInput").ap())
    out = nc.dram_tensor("out_t", (P, KD, S), F32, kind="ExternalOutput").ap()
    two_blocks_kernel(nc, *args, out)
    r = _run(nc, [arrays], core_ids=[0])
    got = np.asarray(r.results[0]["out_t"]).reshape(P, KD, S)
    return got.transpose(2, 1, 0).reshape(1, S, D)
```
